# Optimizing a Trainium2 kernel written in Bass

```python
import math
import jax, jax.numpy as jnp
from jax import lax
import numpy as np

D_MODEL = 1024
BATCH = 1
SEQ = 256
DEPTH = 2

EXPAND = 2
MIX_W = EXPAND * D_MODEL
A_W = MIX_W // 2
B_W = MIX_W - A_W
POOL_WINDOWS = (2, 4, 8, 16)
POOL_GROUPS = len(POOL_WINDOWS)
POOL_CH = A_W // POOL_GROUPS
CONV_K = 31
IN0_W = A_W + 2 * B_W + MIX_W

HEAD_DIM = 64
N_HEADS = D_MODEL // HEAD_DIM
ATT_W = N_HEADS * HEAD_DIM
IN1_W = 4 * ATT_W
MOBA_BLOCK = 256
MOBA_TOPK = 3
Q_CHUNK = 32

N_EVEN = (DEPTH + 1) // 2
N_ODD = DEPTH // 2
EPS = 1e-6

kernel_name = "hybrid_pool_conformer_moba_block"

def rms_norm(x, g):
    xf = x.astype(jnp.float32)
    y = xf * lax.rsqrt(jnp.mean(xf * xf, axis=-1, keepdims=True) + EPS)
    return (y * g.astype(jnp.float32)).astype(x.dtype)

def layer_norm(x, g, b):
    xf = x.astype(jnp.float32)
    mu = jnp.mean(xf, axis=-1, keepdims=True)
    var = jnp.mean(jnp.square(xf - mu), axis=-1, keepdims=True)
    y = (xf - mu) * lax.rsqrt(var + EPS)
    return (y * g.astype(jnp.float32) + b.astype(jnp.float32)).astype(x.dtype)

def alibi_slopes(n_heads):
    return jnp.exp2(-8.0 * jnp.arange(1, n_heads + 1, dtype=jnp.float32) / n_heads)

def multiscale_pool(a):
    B, S, G, C = a.shape
    af = a.astype(jnp.float32)
    cs = jnp.concatenate([jnp.zeros((B, 1, G, C), jnp.float32), jnp.cumsum(af, axis=1)], axis=1)
    t = jnp.arange(S)
    outs = []
    for g, w in enumerate(POOL_WINDOWS):
        lo = jnp.maximum(t + 1 - w, 0)
        win_sum = cs[:, 1:, g] - cs[:, lo, g]
        cnt = (t + 1 - lo).astype(jnp.float32)[None, :, None]
        outs.append(win_sum / cnt - af[:, :, g])
    return jnp.stack(outs, axis=2).astype(a.dtype)

def pool_conv_layer(x, norm_g, w_in, pool_w, pool_scale, conv_w, conv_b, cn_g, cn_b, w_out):
    B, S, _ = x.shape
    h = rms_norm(x, norm_g)
    proj = jnp.einsum('bsd,de->bse', h, w_in)
    a, bv, bg, z = jnp.split(proj, [A_W, A_W + B_W, A_W + 2 * B_W], axis=-1)
    pooled = multiscale_pool(a.reshape(B, S, POOL_GROUPS, POOL_CH))
    ya = jnp.einsum('bsgc,gce->bsge', pooled, pool_w).reshape(B, S, A_W) * pool_scale
    u = bv * jax.nn.sigmoid(bg)
    u = lax.conv_general_dilated(u, conv_w[:, None, :], window_strides=(1,),
                                 padding=[(CONV_K - 1, 0)],
                                 dimension_numbers=('NWC', 'WIO', 'NWC'),
                                 feature_group_count=B_W) + conv_b
    yb = jax.nn.silu(layer_norm(u, cn_g, cn_b))
    y = jnp.concatenate([ya, yb], axis=-1) * jax.nn.silu(z)
    return jnp.einsum('bse,ed->bsd', y, w_out)

def moba_attention(q, k, v, slopes):
    B, H, S, dh = q.shape
    nb = -(-S // MOBA_BLOCK)
    s_pad = nb * MOBA_BLOCK
    pad = ((0, 0), (0, 0), (0, s_pad - S), (0, 0))
    kp = jnp.pad(k, pad)
    vp = jnp.pad(v, pad)
    kb = kp.reshape(B, H, nb, MOBA_BLOCK, dh)
    vb = vp.reshape(B, H, nb, MOBA_BLOCK, dh)
    kmean = jnp.mean(kb.astype(jnp.float32), axis=3)
    n_sel = min(MOBA_TOPK, nb)
    bi = jnp.arange(B)[:, None, None, None]
    hi = jnp.arange(H)[None, :, None, None]
    blk_off = jnp.arange(MOBA_BLOCK)
    sl = slopes[None, :, None]

    def chunk(ci):
        t0 = ci * Q_CHUNK
        qc = lax.dynamic_slice_in_dim(q, t0, Q_CHUNK, axis=2)
        tpos = t0 + jnp.arange(Q_CHUNK)
        own = t0 // MOBA_BLOCK
        gate = jnp.einsum('bhqd,bhnd->bhqn', qc.astype(jnp.float32), kmean)
        gate = jnp.where(jnp.arange(nb) < own, gate, -jnp.inf)
        _, sel = lax.top_k(gate, n_sel)
        valid = jnp.arange(n_sel) < own
        k_sel = kb[bi, hi, sel]
        v_sel = vb[bi, hi, sel]
        s_sel = jnp.einsum('bhqd,bhqnkd->bhqnk', qc, k_sel).astype(jnp.float32)
        spos = sel[..., None] * MOBA_BLOCK + blk_off
        dist_sel = (tpos[None, None, :, None, None] - spos).astype(jnp.float32)
        s_sel = s_sel - sl[..., None, None] * dist_sel
        s_sel = jnp.where(valid[None, None, None, :, None], s_sel, -jnp.inf)
        s_sel = s_sel.reshape(B, H, Q_CHUNK, n_sel * MOBA_BLOCK)
        k_own = lax.dynamic_slice_in_dim(kp, own * MOBA_BLOCK, MOBA_BLOCK, axis=2)
        v_own = lax.dynamic_slice_in_dim(vp, own * MOBA_BLOCK, MOBA_BLOCK, axis=2)
        s_own = jnp.einsum('bhqd,bhkd->bhqk', qc, k_own).astype(jnp.float32)
        dist_own = tpos[:, None] - (own * MOBA_BLOCK + blk_off)[None, :]
        s_own = jnp.where(dist_own >= 0, s_own - sl[..., None] * dist_own.astype(jnp.float32), -jnp.inf)
        p = jax.nn.softmax(jnp.concatenate([s_sel, s_own], axis=-1), axis=-1).astype(v.dtype)
        p_sel = p[..., : n_sel * MOBA_BLOCK].reshape(B, H, Q_CHUNK, n_sel, MOBA_BLOCK)
        p_own = p[..., n_sel * MOBA_BLOCK:]
        o = jnp.einsum('bhqnk,bhqnkd->bhqd', p_sel, v_sel) + jnp.einsum('bhqk,bhkd->bhqd', p_own, v_own)
        return o.astype(q.dtype)

    outs = lax.map(chunk, jnp.arange(S // Q_CHUNK))
    return outs.transpose(1, 2, 0, 3, 4).reshape(B, H, S, dh)

def moba_layer(x, norm_g, w_in, q_norm_g, k_norm_g, w_out):
    B, S, _ = x.shape
    h = rms_norm(x, norm_g)
    proj = jnp.einsum('bsd,de->bse', h, w_in)
    q, k, v, z = jnp.split(proj, 4, axis=-1)
    to_heads = lambda t: t.reshape(B, S, N_HEADS, HEAD_DIM).transpose(0, 2, 1, 3)
    q = rms_norm(to_heads(q), q_norm_g) * (HEAD_DIM ** -0.5)
    k = rms_norm(to_heads(k), k_norm_g)
    o = moba_attention(q, k, to_heads(v), alibi_slopes(N_HEADS))
    o = o.transpose(0, 2, 1, 3).reshape(B, S, ATT_W)
    return jnp.einsum('bse,ed->bsd', o * jax.nn.silu(z), w_out)

def setup_inputs(seed: int = 0) -> dict:
    key = jax.random.key(seed)
    ks = jax.random.split(key, 20)
    f32 = jnp.float32
    nrm = lambda k, shape, scale: jax.random.normal(k, shape, f32) * scale
    return {
        "x": nrm(ks[0], (BATCH, SEQ, D_MODEL), 1.0),
        "norm0_g": 1.0 + nrm(ks[1], (N_EVEN, D_MODEL), 0.05),
        "w_in0": nrm(ks[2], (N_EVEN, D_MODEL, IN0_W), D_MODEL ** -0.5),
        "pool_w": nrm(ks[3], (N_EVEN, POOL_GROUPS, POOL_CH, POOL_CH), POOL_CH ** -0.5),
        "pool_scale": 1.0 + nrm(ks[4], (N_EVEN, A_W), 0.1),
        "conv_w": nrm(ks[5], (N_EVEN, CONV_K, B_W), CONV_K ** -0.5),
        "conv_b": nrm(ks[6], (N_EVEN, B_W), 0.02),
        "cnorm_g": 1.0 + nrm(ks[7], (N_EVEN, B_W), 0.05),
        "cnorm_b": nrm(ks[8], (N_EVEN, B_W), 0.02),
        "w_out0": nrm(ks[9], (N_EVEN, MIX_W, D_MODEL), 0.5 * MIX_W ** -0.5),
        "norm1_g": 1.0 + nrm(ks[10], (N_ODD, D_MODEL), 0.05),
        "w_in1": nrm(ks[11], (N_ODD, D_MODEL, IN1_W), D_MODEL ** -0.5),
        "q_norm_g": 1.0 + nrm(ks[12], (N_ODD, HEAD_DIM), 0.05),
        "k_norm_g": 1.0 + nrm(ks[13], (N_ODD, HEAD_DIM), 0.05),
        "w_out1": nrm(ks[14], (N_ODD, ATT_W, D_MODEL), 0.5 * ATT_W ** -0.5),
    }

def reference(x, norm0_g, w_in0, pool_w, pool_scale, conv_w, conv_b, cnorm_g, cnorm_b, w_out0,
              norm1_g, w_in1, q_norm_g, k_norm_g, w_out1):
    for layer in range(DEPTH):
        i = layer // 2
        if layer % 2 == 0:
            x = x + pool_conv_layer(x, norm0_g[i], w_in0[i], pool_w[i], pool_scale[i], conv_w[i],
                                    conv_b[i], cnorm_g[i], cnorm_b[i], w_out0[i])
        else:
            x = x + moba_layer(x, norm1_g[i], w_in1[i], q_norm_g[i], k_norm_g[i], w_out1[i])
    return x


_drawn_inputs = setup_inputs


def setup_inputs(seed=0):
    import zlib

    import numpy as np

    out = dict(_drawn_inputs(seed))
    spreads = {}
    factors = {'norm0_g': 3.293,
     'pool_scale': 3.115,
     'conv_b': 8.0,
     'cnorm_g': 7.703,
     'cnorm_b': 8.0,
     'norm1_g': 6.1,
     'q_norm_g': 8.0,
     'k_norm_g': 8.0}
    for name, (base, spread) in spreads.items():
        noise = np.random.default_rng([zlib.crc32(name.encode()), seed]).standard_normal(out[name].shape)
        drawn = base * np.exp(spread * noise) if base else spread * noise
        out[name] = __import__('jax').numpy.asarray(drawn.astype(out[name].dtype))
    for name, factor in factors.items():
        out[name] = (out[name] * factor).astype(out[name].dtype)
    return out
```

```python
from contextlib import ExitStack

import concourse.bass as bass
from concourse import mybir

F32 = mybir.dt.float32
F32R = mybir.dt.float32r
ALU = mybir.AluOpType
ACT = mybir.ActivationFunctionType
AX_X = mybir.AxisListType.X

P = 128
S = 256
D = 1024
KD = D // P
TT = S // P
HEADS, DH = 16, 64
TAPS = 31
PAD = TAPS - 1
EPS = 1e-6
UNIT = 2048
UC = UNIT // KD
WINDOWS = (2, 4, 8, 16)
APAD = 16
FAR = 1.0e30

BG = [2 * i for i in range(4)]
BV = [2 * i + 1 for i in range(4)]
A = [8 + g for g in range(4)]
ZB = [12 + i for i in range(4)]
PW = 16
ZA = [17 + i for i in range(4)]
OA = [21 + i for i in range(4)]
OB = [25 + i for i in range(4)]
Z1 = [29 + i for i in range(4)]
KU = [33 + 3 * j for j in range(4)]
QU = [34 + 3 * j for j in range(4)]
VU = [35 + 3 * j for j in range(4)]
O1 = [45 + i for i in range(4)]
NU = 49

NATIVE = frozenset((3, 5, 7, 9, 11, 13, 15, 17, 19))
RAW = 4
CUT = 3

G0, PS, CB, CG, CBETA, G1 = (8 * i for i in range(6))
GQ, GK = 48, 49
CW = 50
NV = CW + KD * TAPS
IC = 0
DIST = IC + 4 * 15
IDN = DIST + 384
QSC = IDN + P
NC = QSC + KD


def cut_index(n):
    return sum(1 for m in range(n) if m not in NATIVE)


CUTS = [n for n in range(NU) if n not in NATIVE]

STEPS = 24
S_AT = [6 * i + 2 for i in range(4)]
T_AT = [6 * i + 10 for i in range(4)]
V_AT = [6 * i + 13 for i in range(4)]
KT_AT, QT_AT = 12, 20
TAPS_PER_SLOT = 11


def hybrid_trunk(nc, xT, w, vec, const, out):
    with ExitStack() as ctx:
        def sb(name, shape, dt=F32):
            return ctx.enter_context(nc.sbuf_tensor(name, shape, dt))

        def sem(name):
            return ctx.enter_context(nc.semaphore(name))

        raw = sb("raw", [P, RAW, UNIT])
        w_hi = sb("w_hi", [P, CUT, UNIT], F32R)
        w_lo = sb("w_lo", [P, CUT, UNIT], F32R)
        X = sb("X", [P, KD, S])
        H = sb("H", [P, KD, S])
        h_hi = sb("h_hi", [P, KD, S], F32R)
        h_lo = sb("h_lo", [P, KD, S], F32R)
        ya_hi = sb("ya_hi", [P, KD, S], F32R)
        ya_lo = sb("ya_lo", [P, KD, S], F32R)
        yb_hi = sb("yb_hi", [P, KD, S], F32R)
        yb_lo = sb("yb_lo", [P, KD, S], F32R)
        SQ = sb("SQ", [P, 2, 2 * S])
        root = sb("root", [P, S])
        rinv = sb("rinv", [P, S])
        V_ = sb("params", [P, NV])
        C_ = sb("consts", [P, NC])
        ones = sb("ones", [P, P])
        eps = sb("eps", [P, 1])
        qscale = sb("qscale", [P, KD])
        ident = C_[:, IDN:IDN + P]
        dist = C_[:, DIST:DIST + 384]

        scratch = sb("scratch", [P, 12800])
        at = 0

        def part(n):
            nonlocal at
            v = scratch[:, at:at + n]
            at += n
            return v

        U = part(KD * (PAD + S)).rearrange("p (c t) -> p c t", c=KD)
        V = part(KD * S).rearrange("p (c t) -> p c t", c=KD)
        SZ = part(2 * KD * S).rearrange("p (c t) -> p c t", c=2 * KD)
        YP = part(KD * S).rearrange("p (c t) -> p c t", c=KD)
        SG = part(2 * S)
        AP = part(2 * (APAD + S)).rearrange("p (c t) -> p c t", c=2)
        W1 = part(2 * (APAD + S)).rearrange("p (c t) -> p c t", c=2)
        W2 = part(2 * (APAD + S)).rearrange("p (c t) -> p c t", c=2)
        FX = part(2 * 15).rearrange("p (c t) -> p c t", c=2)
        assert at <= 12800
        at = 0
        SZ1 = part(KD * S).rearrange("p (c t) -> p c t", c=KD)
        qT = part(4 * S).rearrange("p (b c t) -> p b c t", b=2, c=2)
        kT = part(4 * S).rearrange("p (b c t) -> p b c t", b=2, c=2)
        vv = part(4 * S).rearrange("p (b t c) -> p b t c", b=2, t=2)
        qn = part(4 * S).rearrange("p (b t c) -> p b t c", b=2, t=2)
        sq1 = part(2 * S)
        neg = part(2 * 384).rearrange("p (b c) -> p b c", b=2)
        prob = part(2 * 384).rearrange("p (b c) -> p b c", b=2)
        pT = part(2 * 384).rearrange("p (b c) -> p b c", b=2)
        oz = part(2 * S).rearrange("p (b c) -> p b c", b=2)
        ss = part(2 * 8).rearrange("p (b c) -> p b c", b=2)
        sr = part(2 * 8).rearrange("p (b c) -> p b c", b=2)
        si = part(2 * 8).rearrange("p (b c) -> p b c", b=2)
        nmax = part(2 * 2).rearrange("p (b c) -> p b c", b=2)
        den = part(2 * 2).rearrange("p (b c) -> p b c", b=2)
        rden = part(2 * 2).rearrange("p (b c) -> p b c", b=2)
        assert at <= 12800

        bank = [ctx.enter_context(nc.psum_tensor(f"bank{i}", [P, 512], F32)) for i in range(8)]
        TR, SC, PV = bank[4], (bank[5], bank[6]), bank[7]

        x_in, vec_in, const_in, stored = sem("x_in"), sem("vec_in"), sem("const_in"), sem("stored")
        raw_in = [sem(f"raw_in{i}") for i in range(RAW)]
        ones_set, pads_set, qs_set = sem("ones_set"), sem("pads_set"), sem("qs_set")
        hi_cut, lo_cut = sem("hi_cut"), sem("lo_cut")
        unit_done = sem("unit_done")
        sq_ready, sq_used = sem("sq_ready"), sem("sq_used")
        rms_sum = sem("rms_sum")
        root_ready, rinv_ready = sem("root_ready"), sem("rinv_ready")
        h_ready, hhi_ready, hlo_ready = sem("h_ready"), sem("hhi_ready"), sem("hlo_ready")
        sig_ready, u_ready = sem("sig_ready"), sem("u_ready")
        a_ready, win, pooled, phi_ready, plo_ready = (
            sem("a_ready"), sem("win"), sem("pooled"), sem("phi_ready"), sem("plo_ready"))
        sz_ready, yp_ready = sem("sz_ready"), sem("yp_ready")
        ya_ready, yahi_ready, yalo_ready = sem("ya_ready"), sem("yahi_ready"), sem("yalo_ready")
        tap = sem("tap")
        mean_sum, centred, normed, swished = sem("mean_sum"), sem("centred"), sem("normed"), sem("swished")
        yb_ready, ybhi_ready, yblo_ready = sem("yb_ready"), sem("ybhi_ready"), sem("yblo_ready")
        bank_closed, x_updated = sem("bank_closed"), sem("x_updated")
        sz1_ready = sem("sz1_ready")
        qk_sq, qk_ss, qk_sr, qk_si, qk_normed = (
            sem("qk_sq"), sem("qk_ss"), sem("qk_sr"), sem("qk_si"), sem("qk_normed"))
        qk_turned, qk_out, v_out = sem("qk_turned"), sem("qk_out"), sem("v_out")
        scored, neg_ready, exped, rden_ready, prob_ready = (
            sem("scored"), sem("neg_ready"), sem("exped"), sem("rden_ready"), sem("prob_ready"))
        p_turned, p_out, pv_done, oz_ready, ozhi_ready, ozlo_ready = (
            sem("p_turned"), sem("p_out"), sem("pv_done"), sem("oz_ready"), sem("ozhi_ready"), sem("ozlo_ready"))

        block = ctx.enter_context(nc.Block())

        def column(c, n=1):
            return V_[:, c:c + n]

        def halves(t, slot, half):
            return t[:, slot, half * (UNIT // 2):(half + 1) * (UNIT // 2)]

        @block.sync
        def _(sp):
            sp.dma_start(X[:, :, :], xT).then_inc(x_in, 16)
            for n in range(NU):
                m = n - RAW
                if m >= 0:
                    if m in NATIVE:
                        sp.wait_ge(unit_done, m + 1)
                    else:
                        sp.wait_ge(lo_cut, 2 * cut_index(m) + 2)
                sp.dma_start(raw[:, n % RAW, :], w[n, :, :]).then_inc(raw_in[n % RAW], 16)
                if n == 0:
                    sp.dma_start(V_[:, :], vec).then_inc(vec_in, 16)
                if n == 3:
                    sp.dma_start(C_[:, :], const).then_inc(const_in, 16)
            for m in range(4):
                sp.wait_ge(x_updated, 4 + m + 1)
                sp.dma_start(out[:, 2 * m:2 * m + 2, :], X[:, 2 * m:2 * m + 2, :]).then_inc(stored, 16)
            sp.wait_ge(stored, 64)

        @block.gpsimd
        def _(pool):
            nc.gpsimd.memset(ones[:, :], 1.0 / D).then_inc(ones_set, 1)
            nc.gpsimd.memset(eps[:, :], EPS).then_inc(ones_set, 1)
            nc.gpsimd.memset(U[:, :, 0:PAD], 0.0).then_inc(pads_set, 1)
            nc.gpsimd.memset(AP[:, :, 0:APAD], 0.0).then_inc(pads_set, 1)
            pool.wait_ge(vec_in, 16)
            pool.wait_ge(const_in, 16)
            pool.wait_ge(pads_set, 2)
            nc.gpsimd.tensor_tensor(qscale[:, :], C_[:, QSC:QSC + KD], column(GQ).to_broadcast([P, KD]),
                                    ALU.mult).then_inc(qs_set, 1)

        @block.scalar
        def _(act):
            def cut_hi(n):
                if n >= NU or n in NATIVE:
                    return
                s = cut_index(n)
                act.wait_ge(raw_in[n % RAW], 16 * (n // RAW + 1))
                if s >= CUT:
                    act.wait_ge(unit_done, CUTS[s - CUT] + 1)
                for half in range(2):
                    nc.scalar.copy(halves(w_hi, s % CUT, half), halves(raw, n % RAW, half)).then_inc(hi_cut, 1)

            def square(group, m, source):
                if m >= 2:
                    act.wait_ge(sq_used, 3 * group + m - 1)
                elif m == 1 and group >= 1:
                    act.wait_ge(rms_sum, group)
                elif group >= 1:
                    act.wait_ge(sq_used, 3 * group)
                nc.scalar.activation(SQ[:, m % 2, :], source[:, 2 * m:2 * m + 2, :], ACT.Square).then_inc(sq_ready, 1)

            def rms_squares(group, layer):
                for m in range(4):
                    if layer == 0:
                        if m == 0:
                            act.wait_ge(x_in, 16)
                    else:
                        act.wait_ge(x_updated, m + 1)
                    square(group, m, X)

            def take_root(source, n):
                act.wait_ge(rms_sum, n)
                nc.scalar.activation(root[:, :], source[:, 0:S], ACT.Sqrt, bias=eps[:, 0:1]).then_inc(root_ready, 1)

            def cut_h(layer):
                for k in range(KD):
                    act.wait_ge(h_ready, KD * layer + k + 1)
                    nc.scalar.copy(h_hi[:, k, :], H[:, k, :]).then_inc(hhi_ready, 1)

            act.wait_ge(ones_set, 2)
            rms_squares(0, 0)
            take_root(bank[4], 1)
            cut_hi(0)
            cut_h(0)
            cut_hi(1)

            for n in range(OA[0] + 1):
                cut_hi(n + 2)
                if n - 1 in ZA:
                    i = n - 1 - ZA[0]
                    act.wait_ge(ya_ready, i + 1)
                    nc.scalar.copy(ya_hi[:, 2 * i:2 * i + 2, :], SZ[:, 2 * i:2 * i + 2, :]).then_inc(yahi_ready, 1)
                if n in BG:
                    i = n // 2
                    act.wait_ge(unit_done, n + 1)
                    if i >= 1:
                        act.wait_ge(u_ready, i)
                    nc.scalar.activation(SG[:, :], bank[n % 4][:, :], ACT.Sigmoid).then_inc(sig_ready, 1)
                if n in A:
                    g = n - A[0]
                    act.wait_ge(unit_done, n + 1)
                    if g == 0:
                        act.wait_ge(pads_set, 2)
                    else:
                        act.wait_ge(pooled, g)
                    nc.scalar.copy(AP[:, :, APAD:APAD + S],
                                   bank[n % 4][:, :].rearrange("p (c t) -> p c t", c=2)).then_inc(a_ready, 1)
                if n in ZB or n in ZA:
                    i = n - ZB[0] if n in ZB else n - ZA[0]
                    c = (KD if n in ZB else 0) + 2 * i
                    act.wait_ge(unit_done, n + 1)
                    nc.scalar.activation(SZ[:, c:c + 2, :], bank[n % 4][:, :].rearrange("p (c t) -> p c t", c=2),
                                         ACT.Silu).then_inc(sz_ready, 1)
                if n in ZB:
                    g = n - ZB[0]
                    act.wait_ge(pooled, g + 1)
                    nc.scalar.copy(yb_hi[:, 2 * g:2 * g + 2, :], YP[:, 2 * g:2 * g + 2, :]).then_inc(phi_ready, 1)
                if n == PW:
                    act.wait_ge(unit_done, n + 1)
                    act.wait_ge(plo_ready, 4)
                    for e in range(KD):
                        nc.scalar.mul(YP[:, e, :], bank[4 + e // 2][:, S * (e % 2):S * (e % 2) + S],
                                      column(PS + e)).then_inc(yp_ready, 1)

            cut_hi(OA[0] + 3)
            for m in range(4):
                act.wait_ge(centred, m + 1)
                square(1, m, V)
            take_root(bank[1], 2)
            for m in range(4):
                for c in (2 * m, 2 * m + 1):
                    act.wait_ge(normed, m + 1)
                    nc.scalar.activation(V[:, c, :], V[:, c, :], ACT.Silu, bias=column(CBETA + c),
                                         scale=column(CG + c)).then_inc(swished, 1)
                if m >= 1:
                    act.wait_ge(yb_ready, m)
                    nc.scalar.copy(yb_hi[:, 2 * m - 2:2 * m, :], SZ[:, KD + 2 * m - 2:KD + 2 * m, :]).then_inc(ybhi_ready, 1)
            act.wait_ge(yb_ready, 4)
            nc.scalar.copy(yb_hi[:, 6:8, :], SZ[:, KD + 6:KD + 8, :]).then_inc(ybhi_ready, 1)
            for n in range(OA[0] + 4, Z1[0] + 2):
                cut_hi(n)

            rms_squares(2, 1)
            take_root(bank[0], 3)
            cut_h(1)

            def head_exp(h):
                for t, (a, b) in enumerate(((0, 128), (128, 384))):
                    act.wait_ge(neg_ready, 2 * h + t + 1)
                    if h >= 2 and t == 0:
                        act.wait_ge(p_turned, h - 1)
                    nc.scalar.activation(prob[:, h % 2, a:b], neg[:, h % 2, a:b], ACT.Exp, scale=-1.0,
                                         bias=nmax[:, h % 2, t:t + 1],
                                         accum_out=den[:, h % 2, t:t + 1]).then_inc(exped, 1)

            def head_turn_out(h):
                act.wait_ge(p_turned, h + 1)
                if h >= 2:
                    act.wait_ge(pv_done, h - 1)
                nc.scalar.copy(pT[:, h % 2, :], TR[:, 0:384]).then_inc(p_out, 1)

            def heads_hi(pair):
                act.wait_ge(oz_ready, pair + 1)
                nc.scalar.copy(ya_hi[:, pair, :], oz[:, pair % 2, :]).then_inc(ozhi_ready, 1)

            def attention_step(j, s):
                for i in range(4):
                    if 0 <= j < 4 and s == S_AT[i] + 1:
                        head_exp(4 * j + i)
                    if 0 <= j < 4 and s == T_AT[i]:
                        head_turn_out(4 * j + i)
                    if j >= 1 and s == T_AT[i] - STEPS:
                        head_turn_out(4 * (j - 1) + i)
                if 0 <= j < 4 and s == V_AT[1] + 2:
                    heads_hi(2 * j)
                if j >= 1 and s == V_AT[3] + 2 - STEPS:
                    heads_hi(2 * j - 1)

            for n in Z1:
                cut_hi(n + 2)
                act.wait_ge(unit_done, n + 1)
                i = n - Z1[0]
                nc.scalar.activation(SZ1[:, 2 * i:2 * i + 2, :], bank[n % 4][:, :].rearrange("p (c t) -> p c t", c=2),
                                     ACT.Silu).then_inc(sz1_ready, 1)

            def qk_norm(n, j, isq):
                r = 2 * j + isq
                act.wait_ge(unit_done, n + 1)
                if r >= 1:
                    act.wait_ge(qk_ss, r)
                nc.scalar.activation(sq1[:, :], bank[n % 4][:, :], ACT.Square, scale=DH ** -0.5).then_inc(qk_sq, 1)
                act.wait_ge(qk_ss, r + 1)
                nc.scalar.activation(sr[:, isq, :], ss[:, isq, :], ACT.Sqrt, bias=eps[:, 0:1]).then_inc(qk_sr, 1)

            def qk_turn_out(j, isq):
                r = 2 * j + isq
                act.wait_ge(qk_turned, r + 1)
                if isq:
                    act.wait_ge(qs_set, 1)
                for c in range(2):
                    nc.scalar.mul((qT if isq else kT)[:, j % 2, c, :], TR[:, c * S:c * S + S],
                                  qscale[:, 2 * j + c:2 * j + c + 1] if isq else column(GK)).then_inc(qk_out, 1)

            for j in range(4):
                for u, n in enumerate((KU[j], QU[j], VU[j])):
                    for step in range(8):
                        s = 8 * u + step
                        attention_step(j - 1, s)
                        if step == 2:
                            cut_hi(n + 2)
                        if s == KT_AT:
                            qk_turn_out(j, 0)
                        if s == QT_AT:
                            qk_turn_out(j, 1)
                    if u < 2:
                        qk_norm(n, j, u)
                    else:
                        act.wait_ge(unit_done, n + 1)
                        if j >= 2:
                            act.wait_ge(pv_done, 4 * (j - 1))
                        nc.scalar.copy(vv[:, j % 2, :, :], bank[n % 4][:, :].rearrange("p (t c) -> p t c", t=2)
                                       ).then_inc(v_out, 1)
            for s in range(STEPS + 10):
                attention_step(3 if s < STEPS else 4, s % STEPS)
                if s == 2:
                    cut_hi(O1[0] + 2)
                if s == 10:
                    cut_hi(O1[0] + 3)

        @block.vector
        def _(dve):
            def cut_lo(n):
                if n >= NU or n in NATIVE:
                    return
                s = cut_index(n)
                for half in range(2):
                    dve.wait_ge(hi_cut, 2 * s + half + 1)
                    nc.vector.tensor_tensor(halves(w_lo, s % CUT, half), halves(raw, n % RAW, half),
                                            halves(w_hi, s % CUT, half).bitcast(F32), ALU.subtract).then_inc(lo_cut, 1)

            def normed_h(layer):
                g = (G0, G1)[layer]
                root_count = 1 if layer == 0 else 3
                dve.wait_ge(root_ready, root_count)
                nc.vector.reciprocal(rinv[:, :], root[:, :]).then_inc(rinv_ready, 1)
                dve.wait_ge(rinv_ready, root_count)
                if layer == 0:
                    dve.wait_ge(vec_in, 16)
                for k in range(KD + 1):
                    if k < KD:
                        nc.vector.scalar_tensor_tensor(H[:, k, :], X[:, k, :], column(g + k), rinv[:, :],
                                                       ALU.mult, ALU.mult).then_inc(h_ready, 1)
                    if k >= 1:
                        dve.wait_ge(hhi_ready, KD * layer + k)
                        nc.vector.tensor_tensor(h_lo[:, k - 1, :], H[:, k - 1, :], h_hi[:, k - 1, :].bitcast(F32),
                                                ALU.subtract).then_inc(hlo_ready, 1)

            normed_h(0)
            cut_lo(0)
            cut_lo(1)

            def window_sums(g):
                width = WINDOWS[g]
                dve.wait_ge(a_ready, g + 1)
                src = AP
                count = sum(lv + 2 for lv in range(g))
                for lv in range(g + 1):
                    shift = 1 << lv
                    lo = APAD if lv == g else 2 * shift
                    dst = (W1, W2)[lv % 2]
                    if lv:
                        dve.wait_ge(win, count + lv)
                    nc.vector.tensor_tensor(dst[:, :, lo:APAD + S], src[:, :, lo:APAD + S],
                                            src[:, :, lo - shift:APAD + S - shift], ALU.add).then_inc(win, 1)
                    src = dst
                dve.wait_ge(win, count + g + 1)
                F = width - 1
                inv = C_[:, IC + 15 * g:IC + 15 * g + F].unsqueeze(1).to_broadcast([P, 2, F])
                nc.vector.scalar_tensor_tensor(YP[:, 2 * g:2 * g + 2, F:S], src[:, :, APAD + F:APAD + S], 1.0 / width,
                                               AP[:, :, APAD + F:APAD + S], ALU.mult, ALU.subtract)
                if g == 0:
                    dve.wait_ge(const_in, 16)
                nc.vector.tensor_tensor(FX[:, :, 0:F], src[:, :, APAD:APAD + F], inv, ALU.mult).then_inc(win, 1)
                dve.wait_ge(win, count + g + 2)
                nc.vector.tensor_tensor(YP[:, 2 * g:2 * g + 2, 0:F], FX[:, :, 0:F], AP[:, :, APAD:APAD + F],
                                        ALU.subtract).then_inc(pooled, 1)

            done = 0

            def taps(count, ready):
                nonlocal done
                for _ in range(count):
                    pair, rest = divmod(done, 2 * TAPS)
                    if pair >= ready:
                        return
                    k, b = divmod(rest, 2)
                    c = 2 * pair + b
                    src = U[:, c, k:k + S]
                    wk = column(CW + TAPS * c + k)
                    if k == 0:
                        if b == 0:
                            dve.wait_ge(u_ready, pair + 1)
                        nc.vector.tensor_scalar(V[:, c, :], src, wk, column(CB + c), ALU.mult, ALU.add).then_inc(tap, 1)
                    else:
                        dve.wait_ge(tap, done - 1)
                        nc.vector.scalar_tensor_tensor(V[:, c, :], src, wk, V[:, c, :],
                                                       ALU.mult, ALU.add).then_inc(tap, 1)
                    done += 1

            dve.wait_ge(pads_set, 2)
            for n in range(OA[0] + 1):
                cut_lo(n + 2)
                m = n - 1
                if m in BV:
                    i = m // 2
                    dve.wait_ge(sig_ready, i + 1)
                    dve.wait_ge(unit_done, m + 1)
                    nc.vector.tensor_tensor(U[:, 2 * i:2 * i + 2, PAD:PAD + S],
                                            bank[m % 4][:, :].rearrange("p (c t) -> p c t", c=2),
                                            SG[:, :].rearrange("p (c t) -> p c t", c=2), ALU.mult).then_inc(u_ready, 1)
                if m in A:
                    window_sums(m - A[0])
                if m in ZB:
                    g = m - ZB[0]
                    dve.wait_ge(phi_ready, g + 1)
                    nc.vector.tensor_tensor(yb_lo[:, 2 * g:2 * g + 2, :], YP[:, 2 * g:2 * g + 2, :],
                                            yb_hi[:, 2 * g:2 * g + 2, :].bitcast(F32), ALU.subtract).then_inc(plo_ready, 1)
                if m in ZA:
                    i = m - ZA[0]
                    dve.wait_ge(sz_ready, 4 + i + 1)
                    dve.wait_ge(yp_ready, 2 * i + 2)
                    nc.vector.tensor_tensor(SZ[:, 2 * i:2 * i + 2, :], SZ[:, 2 * i:2 * i + 2, :],
                                            YP[:, 2 * i:2 * i + 2, :], ALU.mult).then_inc(ya_ready, 1)
                taps(TAPS_PER_SLOT, (m + 1) // 2)
                if m in ZA:
                    dve.wait_ge(yahi_ready, i + 1)
                    nc.vector.tensor_tensor(ya_lo[:, 2 * i:2 * i + 2, :], SZ[:, 2 * i:2 * i + 2, :],
                                            ya_hi[:, 2 * i:2 * i + 2, :].bitcast(F32), ALU.subtract).then_inc(yalo_ready, 1)
            cut_lo(OA[0] + 3)
            taps(2 * TAPS * 4, 4)
            assert done == TAPS * KD

            dve.wait_ge(mean_sum, 1)
            for m in range(4):
                nc.vector.tensor_tensor(V[:, 2 * m:2 * m + 2, :], V[:, 2 * m:2 * m + 2, :],
                                        bank[0][:, 0:S].unsqueeze(1).to_broadcast([P, 2, S]),
                                        ALU.subtract).then_inc(centred, 1)
            dve.wait_ge(root_ready, 2)
            nc.vector.reciprocal(rinv[:, :], root[:, :]).then_inc(rinv_ready, 1)
            dve.wait_ge(rinv_ready, 2)
            dve.wait_ge(sq_ready, 8)
            for m in range(4):
                nc.vector.tensor_tensor(V[:, 2 * m:2 * m + 2, :], V[:, 2 * m:2 * m + 2, :],
                                        rinv[:, :].unsqueeze(1).to_broadcast([P, 2, S]), ALU.mult).then_inc(normed, 1)
            dve.wait_ge(sz_ready, 8)
            for m in range(5):
                if m < 4:
                    dve.wait_ge(swished, 2 * m + 2)
                    nc.vector.tensor_tensor(SZ[:, KD + 2 * m:KD + 2 * m + 2, :], SZ[:, KD + 2 * m:KD + 2 * m + 2, :],
                                            V[:, 2 * m:2 * m + 2, :], ALU.mult).then_inc(yb_ready, 1)
                if m >= 1:
                    dve.wait_ge(ybhi_ready, m)
                    nc.vector.tensor_tensor(yb_lo[:, 2 * m - 2:2 * m, :], SZ[:, KD + 2 * m - 2:KD + 2 * m, :],
                                            yb_hi[:, 2 * m - 2:2 * m, :].bitcast(F32), ALU.subtract).then_inc(yblo_ready, 1)
            for n in range(OA[0] + 4, Z1[0] + 2):
                cut_lo(n)

            def residual(m, layer):
                if m < 3:
                    dve.wait_ge(bank_closed, 3 * layer + m + 1)
                else:
                    dve.wait_ge(unit_done, (Z1[0], NU)[layer])
                nc.vector.tensor_tensor(X[:, 2 * m:2 * m + 2, :], X[:, 2 * m:2 * m + 2, :],
                                        bank[(4, 0)[layer] + m][:, :].rearrange("p (c t) -> p c t", c=2),
                                        ALU.add).then_inc(x_updated, 1)

            for m in range(4):
                residual(m, 0)
            normed_h(1)

            def head_bias(h):
                slope = 2.0 ** (-8.0 * (h + 1) / HEADS)
                dve.wait_ge(scored, h + 1)
                if h >= 2:
                    dve.wait_ge(exped, 2 * h - 2)
                for t, (a, b) in enumerate(((0, 128), (128, 384))):
                    nc.vector.tensor_tensor_reduce(neg[:, h % 2, a:b], dist[:, a:b], SC[h % 2][:, a:b], slope, 3.0e38,
                                                   ALU.add, ALU.min,
                                                   nmax[:, h % 2, t:t + 1]).then_inc(neg_ready, 1)

            def head_scale(h):
                dve.wait_ge(exped, 2 * h + 2)
                nc.vector.reciprocal(rden[:, h % 2, :], den[:, h % 2, :]).then_inc(rden_ready, 1)
                dve.wait_ge(rden_ready, h + 1)
                for t, (a, b) in enumerate(((0, 128), (128, 384))):
                    nc.vector.tensor_scalar(prob[:, h % 2, a:b], prob[:, h % 2, a:b], rden[:, h % 2, t:t + 1], None,
                                            ALU.mult).then_inc(prob_ready, 1)

            def heads_gate(pair):
                dve.wait_ge(pv_done, 2 * pair + 2)
                if pair >= 2:
                    dve.wait_ge(ozlo_ready, pair - 1)
                    dve.wait_ge(ozhi_ready, pair - 1)
                if pair == 0:
                    dve.wait_ge(sz1_ready, 4)
                nc.vector.tensor_tensor(oz[:, pair % 2, :], PV[:, 0:S], SZ1[:, pair, :], ALU.mult).then_inc(oz_ready, 1)

            def heads_lo(pair):
                dve.wait_ge(ozhi_ready, pair + 1)
                nc.vector.tensor_tensor(ya_lo[:, pair, :], oz[:, pair % 2, :], ya_hi[:, pair, :].bitcast(F32),
                                        ALU.subtract).then_inc(ozlo_ready, 1)

            def attention_step(j, s):
                for i in range(4):
                    if 0 <= j < 4 and s == S_AT[i]:
                        head_bias(4 * j + i)
                    if 0 <= j < 4 and s == S_AT[i] + 3:
                        head_scale(4 * j + i)
                if 0 <= j < 4 and s == V_AT[1] + 1:
                    heads_gate(2 * j)
                if 0 <= j < 4 and s == V_AT[1] + 3:
                    heads_lo(2 * j)
                if j >= 1 and s == V_AT[3] + 1 - STEPS:
                    heads_gate(2 * j - 1)
                if j >= 1 and s == V_AT[3] + 3 - STEPS:
                    heads_lo(2 * j - 1)

            for n in Z1:
                cut_lo(n + 2)
            dve.wait_ge(const_in, 16)

            def qk_norm(n, j, isq):
                r = 2 * j + isq
                src = bank[n % 4][:, :].rearrange("p (h d) -> p h d", d=DH)
                dve.wait_ge(qk_sq, r + 1)
                nc.vector.tensor_reduce(ss[:, isq, :], sq1[:, :].rearrange("p (h d) -> p h d", d=DH),
                                        AX_X, ALU.add).then_inc(qk_ss, 1)
                dve.wait_ge(qk_sr, r + 1)
                nc.vector.reciprocal(si[:, isq, :], sr[:, isq, :]).then_inc(qk_si, 1)
                dve.wait_ge(qk_si, r + 1)
                if r >= 2:
                    dve.wait_ge(qk_turned, r - 1)
                nc.vector.tensor_tensor(qn[:, isq, :, :].rearrange("p t (h d) -> p (t h) d", d=DH), src,
                                        si[:, isq, :].unsqueeze(2).to_broadcast([P, 8, DH]),
                                        ALU.mult).then_inc(qk_normed, 1)

            for j in range(4):
                for u, n in enumerate((KU[j], QU[j], VU[j])):
                    for step in range(8):
                        attention_step(j - 1, 8 * u + step)
                        if step == 2:
                            cut_lo(n + 2)
                    if u < 2:
                        qk_norm(n, j, u)
            for s in range(STEPS + 11):
                attention_step(3 if s < STEPS else 4, s % STEPS)
                if s == 2:
                    cut_lo(O1[0] + 2)
                if s == 10:
                    cut_lo(O1[0] + 3)
            for m in range(4):
                residual(m, 1)

        @block.tensor
        def _(pe):
            def product(dst, stationary, moving, start, stop):
                (wh, wl), (ah, al) = stationary, moving
                nc.tensor.matmul(dst, wh, ah, start=start, stop=False, skip_group_check=True)
                nc.tensor.matmul(dst, wh, al, start=False, stop=False, skip_group_check=True)
                return nc.tensor.matmul(dst, wl, ah, start=False, stop=stop, skip_group_check=True)

            def arrived(n, half):
                if n in NATIVE:
                    if half == 0:
                        pe.wait_ge(raw_in[n % RAW], 16 * (n // RAW + 1))
                else:
                    pe.wait_ge(lo_cut, 2 * cut_index(n) + half + 1)

            def piece(n, a, b):
                s = cut_index(n) % CUT
                return raw[:, n % RAW, a:b], (w_hi[:, s, a:b], w_lo[:, s, a:b])

            def channel_step(n, k, h_wait):
                if k % 4 == 0:
                    arrived(n, k // 4)
                if h_wait is not None:
                    pe.wait_ge(hlo_ready, KD * h_wait + k + 1)
                for c in range(2):
                    a = k * UC + c * P
                    wr, wp = piece(n, a, a + P)
                    dst = bank[n % 4][:, c * S:c * S + S]
                    start, stop = k == 0 and c == 0, k == KD - 1
                    if n in NATIVE:
                        last = nc.tensor.matmul(dst, wr, H[:, k, :], start=start, stop=stop, skip_group_check=True)
                    else:
                        last = product(dst, wp, (h_hi[:, k, :], h_lo[:, k, :]), start, stop)
                if k == KD - 1:
                    last.then_inc(unit_done, 1)

            def token_step(n, k):
                if k % 4 == 0:
                    arrived(n, k // 4)
                _, (wh, wl) = piece(n, k * UC, (k + 1) * UC)
                for t in range(TT):
                    ah, al = h_hi[:, k, t * P:t * P + P], h_lo[:, k, t * P:t * P + P]
                    last = product(bank[n % 4][:, t * UC:t * UC + UC], (ah, al), (wh, wl),
                                   k == 0 and t == 0, k == KD - 1)
                if k == KD - 1:
                    last.then_inc(unit_done, 1)

            def out_product(n, kt, m, y, tile, acc, start, stop):
                a = kt * D + m * P
                wr, wp = piece(n, a, a + P)
                y_hi, y_lo = y
                return product(bank[acc + m // 2][:, S * (m % 2):S * (m % 2) + S], wp,
                               (y_hi[:, tile, :], y_lo[:, tile, :]), start and m % 2 == 0, stop)

            pe.wait_ge(ones_set, 1)

            def rms_sums(first, dst):
                for m in range(4):
                    pe.wait_ge(sq_ready, first + m + 1)
                    nc.tensor.matmul(dst[:, 0:S], ones[:, :], SQ[:, m % 2, 0:S], start=(m == 0), stop=False)
                    nc.tensor.matmul(dst[:, 0:S], ones[:, :], SQ[:, m % 2, S:2 * S], start=False,
                                     stop=(m == 3)).then_inc(rms_sum if m == 3 else sq_used, 1)

            rms_sums(0, bank[4])

            for n in range(PW):
                if n >= 4:
                    m = n - 4
                    if m in BG:
                        pe.wait_ge(sig_ready, m // 2 + 1)
                    elif m in BV:
                        pe.wait_ge(u_ready, m // 2 + 1)
                    elif m in A:
                        pe.wait_ge(a_ready, m - A[0] + 1)
                for k in range(KD):
                    channel_step(n, k, 0 if n == 0 else None)

            n = PW
            for g in range(4):
                if g % 2 == 0:
                    arrived(n, g // 2)
                pe.wait_ge(plo_ready, g + 1)
                if g == 0:
                    pe.wait_ge(root_ready, 1)
                for ct in range(2):
                    for e in range(2):
                        a = (2 * g + ct) * UC + e * P
                        wr, wp = piece(n, a, a + P)
                        last = product(bank[4 + g][:, e * S:e * S + S], wp,
                                       (yb_hi[:, 2 * g + ct, :], yb_lo[:, 2 * g + ct, :]), ct == 0 and e == 0, ct == 1)
            last.then_inc(unit_done, 1)

            for n in ZA:
                if n != ZA[3]:
                    pe.wait_ge(sz_ready, n - ZA[0] + 2)
                for k in range(KD):
                    channel_step(n, k, None)

            pe.wait_ge(yp_ready, KD)
            for i, n in enumerate(OA):
                pe.wait_ge(yalo_ready, i + 1)
                for kt in range(2):
                    arrived(n, kt)
                    for m in range(KD):
                        last = out_product(n, kt, m, (ya_hi, ya_lo), 2 * i + kt, 4, i == 0 and kt == 0, False)
                last.then_inc(unit_done, 1)

            pe.wait_ge(sz_ready, 8)
            pe.wait_ge(tap, KD * TAPS)
            for c in range(KD):
                last = nc.tensor.matmul(bank[0][:, 0:S], ones[:, :], V[:, c, :], start=(c == 0), stop=(c == KD - 1))
            last.then_inc(mean_sum, 1)
            rms_sums(4, bank[1])

            for i in range(2):
                n = OB[i]
                pe.wait_ge(yblo_ready, i + 1)
                for kt in range(2):
                    arrived(n, kt)
                    for m in range(KD):
                        last = out_product(n, kt, m, (yb_hi, yb_lo), 2 * i + kt, 4, False, False)
                last.then_inc(unit_done, 1)

            def closing(units, y, first_tile, acc, ready):
                pe.wait_ge(ready[0], ready[1])
                for n in units:
                    arrived(n, 1)
                for m in range(KD):
                    for u, n in enumerate(units):
                        for kt in range(2):
                            last = out_product(n, kt, m, y, first_tile + 2 * u + kt, acc, False, u == len(units) - 1 and kt == 1)
                        if m == KD - 1 and u == 0 and len(units) == 2:
                            last.then_inc(unit_done, 1)
                    if m % 2 == 1 and m < KD - 1:
                        last.then_inc(bank_closed, 1)
                last.then_inc(unit_done, 1)

            closing(OB[2:], (yb_hi, yb_lo), 4, 4, (yblo_ready, 4))

            rms_sums(8, bank[0])

            for n in Z1:
                if n % 4 == 0:
                    pe.wait_ge(root_ready, 3)
                for k in range(KD):
                    channel_step(n, k, 1 if n == Z1[0] else None)

            def turn_qk(j, isq):
                pe.wait_ge(qk_normed, 2 * j + isq + 1)
                turn_bank_free()
                for c in range(2):
                    for t in range(TT):
                        last = nc.tensor.transpose(TR[:, c * S + t * P:c * S + t * P + P],
                                                   qn[:, isq, t, c * P:c * P + P], ident)
                last.then_inc(qk_turned, 1)

            turned = []

            def turn_bank_free():
                if turned:
                    kind, count = turned[-1]
                    pe.wait_ge(qk_out if kind == "qk" else p_out, count)

            def head_scores(h):
                j, c, r = h // 4, (h // 2) % 2, DH * (h % 2)
                pe.wait_ge(qk_out, 4 * j + 4)
                if h >= 2:
                    pe.wait_ge(neg_ready, 2 * h - 2)
                nc.tensor.matmul(SC[h % 2][:, 0:P], qT[r:r + DH, j % 2, c, 0:P], kT[r:r + DH, j % 2, c, 0:P],
                                 start=True, stop=True, skip_group_check=True)
                nc.tensor.matmul(SC[h % 2][:, P:P + S], qT[r:r + DH, j % 2, c, P:S], kT[r:r + DH, j % 2, c, :],
                                 start=False, stop=True, skip_group_check=True).then_inc(scored, 1)

            def head_turn(h):
                pe.wait_ge(prob_ready, 2 * h + 2)
                turn_bank_free()
                for i, (a, b) in enumerate(((0, 0), (128, 128), (256, 256))):
                    last = nc.tensor.transpose(TR[:, a:a + P], prob[:, h % 2, b:b + P], ident)
                last.then_inc(p_turned, 1)
                turned.append(("p", h + 1))

            def head_values(h):
                j, r = h // 4, DH * (h % 2)
                pe.wait_ge(p_out, h + 1)
                pe.wait_ge(v_out, j + 1)
                if h % 2 == 0 and h >= 2:
                    pe.wait_ge(oz_ready, h // 2)
                a = DH * (h % 4)
                nc.tensor.matmul(PV[r:r + DH, 0:S], vv[:, j % 2, 0, a:a + DH], pT[:, h % 2, 0:S],
                                 start=True, stop=False, skip_group_check=True)
                nc.tensor.matmul(PV[r:r + DH, P:S], vv[:, j % 2, 1, a:a + DH], pT[:, h % 2, S:S + P],
                                 start=False, stop=True, skip_group_check=True).then_inc(pv_done, 1)

            def attention_step(j, s):
                for i in range(4):
                    if 0 <= j < 4 and s == S_AT[i]:
                        head_scores(4 * j + i)
                    if 0 <= j < 4 and s == T_AT[i]:
                        head_turn(4 * j + i)
                    if 0 <= j < 4 and s == V_AT[i]:
                        head_values(4 * j + i)
                    if j >= 1 and s == T_AT[i] - STEPS:
                        head_turn(4 * (j - 1) + i)
                    if j >= 1 and s == V_AT[i] - STEPS:
                        head_values(4 * (j - 1) + i)

            pe.wait_ge(const_in, 16)
            for j in range(4):
                for u, n in enumerate((KU[j], QU[j], VU[j])):
                    m = n - 4
                    if m in Z1:
                        pe.wait_ge(sz1_ready, m - Z1[0] + 1)
                    elif m in VU:
                        pe.wait_ge(v_out, VU.index(m) + 1)
                    else:
                        pe.wait_ge(qk_normed, 2 * ((m - KU[0]) // 3) + (m - KU[0]) % 3 + 1)
                    for k in range(KD):
                        s = 8 * u + k
                        if s == KT_AT:
                            turn_qk(j, 0)
                            turned.append(("qk", 4 * j + 2))
                        if s == QT_AT:
                            turn_qk(j, 1)
                            turned.append(("qk", 4 * j + 4))
                        attention_step(j - 1, s)
                        token_step(n, k)

            pe.wait_ge(v_out, 4)
            pe.wait_ge(qk_normed, 8)
            s = 0
            for i in range(3):
                n = O1[i]
                for kt in range(2):
                    pe.wait_ge(ozlo_ready, 2 * i + kt + 1)
                    arrived(n, kt)
                    for m in range(KD):
                        if m % 2 == 0:
                            attention_step(3, s)
                            s += 1
                        last = out_product(n, kt, m, (ya_hi, ya_lo), 2 * i + kt, 0, i == 0 and kt == 0, False)
                last.then_inc(unit_done, 1)
            while s < STEPS + 8:
                attention_step(3 if s < STEPS else 4, s % STEPS)
                s += 1
            closing(O1[3:], (ya_hi, ya_lo), 6, 0, (ozlo_ready, 8))


def kernel(x, norm0_g, w_in0, pool_w, pool_scale, conv_w, conv_b, cnorm_g, cnorm_b, w_out0,
           norm1_g, w_in1, q_norm_g, k_norm_g, w_out1):
    import numpy as np
    import concourse.bacc as bacc
    from concourse.bass_utils import run_bass_kernel_spmd

    def tiles(v):
        return np.asarray(v).reshape(KD, P).T

    def columns(wt, c):
        return np.asarray(wt)[0][:, c:c + UC].reshape(KD, P, UC).transpose(1, 0, 2).reshape(P, UNIT)

    def rows(wt, i):
        return np.asarray(wt)[0][2 * P * i:2 * P * (i + 1)].reshape(2, P, D).transpose(1, 0, 2).reshape(P, UNIT)

    units = []
    for i in range(4):
        units += [columns(w_in0, 2 * D + UC * i), columns(w_in0, D + UC * i)]
    units += [columns(w_in0, UC * g) for g in range(4)]
    units += [columns(w_in0, 4 * D + UC * i) for i in range(4)]
    units += [np.asarray(pool_w)[0].reshape(4, 2, P, UC).transpose(2, 0, 1, 3).reshape(P, UNIT)]
    units += [columns(w_in0, 3 * D + UC * i) for i in range(4)]
    units += [rows(w_out0, i) for i in range(8)]
    units += [columns(w_in1, 3 * D + UC * i) for i in range(4)]
    for j in range(4):
        units += [columns(w_in1, D + UC * j), columns(w_in1, UC * j), columns(w_in1, 2 * D + UC * j)]
    units += [rows(w_out1, i) for i in range(4)]
    taps = np.asarray(conv_w)[0].reshape(TAPS, KD, P).transpose(2, 1, 0).reshape(P, KD * TAPS)
    twice = [np.concatenate([np.asarray(g)[0]] * 2)[:, None] for g in (q_norm_g, k_norm_g)]
    vec = np.concatenate([tiles(norm0_g), tiles(pool_scale), tiles(conv_b), tiles(cnorm_g), tiles(cnorm_b),
                          tiles(norm1_g)] + twice + [taps], axis=1)
    t = np.arange(15)
    inv = np.concatenate([1.0 / np.minimum(t + 1, wd) for wd in WINDOWS])
    q, k = np.arange(P)[:, None], np.arange(P)[None, :]
    own = np.where(q >= k, q - k, FAR)
    heads = 2 * np.arange(KD)[None, :] + np.arange(P)[:, None] // DH
    scale = -DH ** -0.5 * 2.0 ** (8.0 * (heads + 1) / HEADS)
    const = np.concatenate([np.broadcast_to(inv, (P, 60)), own, q - k + P, own, np.eye(P), scale], axis=1).astype(np.float32)
    arrays = {
        "xT": np.ascontiguousarray(np.asarray(x)[0].T.reshape(KD, P, S).transpose(1, 0, 2)),
        "w": np.ascontiguousarray(np.stack(units)),
        "vec": np.ascontiguousarray(vec),
        "const": const,
    }
    nc = bacc.Bacc("TRN2", target_bir_lowering=False, num_devices=1)
    args = [nc.dram_tensor(n, a.shape, F32, kind="ExternalInput").ap() for n, a in arrays.items()]
    out = nc.dram_tensor("out", (P, KD, S), F32, kind="ExternalOutput").ap()
    hybrid_trunk(nc, *args, out)
    r = run_bass_kernel_spmd(nc, [arrays], core_ids=[0])
    return r.results[0]["out"].transpose(1, 0, 2).reshape(D, S).T[None]
```

```python
from contextlib import ExitStack

import concourse.bass as bass
from concourse import mybir

F32 = mybir.dt.float32
F32R = mybir.dt.float32r
ALU = mybir.AluOpType
ACT = mybir.ActivationFunctionType
AX_X = mybir.AxisListType.X

P = 128
S = 256
D = 1024
KD = D // P
TT = S // P
HEADS, DH = 16, 64
TAPS = 31
PAD = TAPS - 1
EPS = 1e-6
UNIT = 2048
UC = UNIT // KD
WINDOWS = (2, 4, 8, 16)
APAD = 16
FAR = 1.0e30

BG = [2 * i for i in range(4)]
BV = [2 * i + 1 for i in range(4)]
A = [8 + g for g in range(4)]
ZB = [12 + i for i in range(4)]
PW = 16
ZA = [17 + i for i in range(4)]
OA = [21 + i for i in range(4)]
OB = [25 + i for i in range(4)]
Z1 = [29 + i for i in range(4)]
KU = [33 + 3 * j for j in range(4)]
QU = [34 + 3 * j for j in range(4)]
VU = [35 + 3 * j for j in range(4)]
O1 = [45 + i for i in range(4)]
NU = 49

NATIVE = frozenset((3, 5, 7, 9, 11, 13, 15, 17, 19))
WARM = 20
RAW = 4
CUT = 3

G0, PS, CB, CG, CBETA, G1 = (8 * i for i in range(6))
GQ, GK = 48, 49
CW = 50
NV = CW + KD * TAPS
IC = 0
DIST = IC + 4 * 15
IDN = DIST + 384
QSC = IDN + P
NC = QSC + KD


def cut_index(n):
    return sum(1 for m in range(n) if m not in NATIVE)


CUTS = [n for n in range(NU) if n not in NATIVE]

STEPS = 24
CUT_HI_AT, CUT_LO_AT = 2, 5
SUM_AT, NORM_AT = 0, 4
KT_AT, QT_AT = 15, STEPS + 1


def head_steps(j):
    gap, to_turn, to_values, first = (6, 7, 10, 4) if j < 3 else (4, 6, 9, 3)
    scores = [gap * i + first for i in range(4)]
    return scores, [s + to_turn for s in scores], [s + to_values for s in scores]


TAPS_PER_SLOT = 11

CONV_GROUPS = ((0, 1), (2, 3), (4, 5, 6))
CONV_PE = 7
CONV_CUT = 16
CONV_ORDER = [(c, k) for group in CONV_GROUPS for k in range(TAPS) for c in group]

EARLY = (BG[0], BV[0]), (Z1[0], Z1[1])


def hybrid_trunk(nc, xT, w, vec, const, out):
    with ExitStack() as ctx:
        def sb(name, shape, dt=F32):
            return ctx.enter_context(nc.sbuf_tensor(name, shape, dt))

        def sem(name):
            return ctx.enter_context(nc.semaphore(name))

        raw = sb("raw", [P, RAW, UNIT])
        w_hi = sb("w_hi", [P, CUT, UNIT], F32R)
        w_lo = sb("w_lo", [P, CUT, UNIT], F32R)
        X = sb("X", [P, KD, S])
        H = sb("H", [P, KD, S])
        h_hi = sb("h_hi", [P, KD, S], F32R)
        h_lo = sb("h_lo", [P, KD, S], F32R)
        ya_hi = sb("ya_hi", [P, KD, S], F32R)
        ya_lo = sb("ya_lo", [P, KD, S], F32R)
        yb_hi = sb("yb_hi", [P, KD, S], F32R)
        yb_lo = sb("yb_lo", [P, KD, S], F32R)
        SQ = sb("SQ", [P, 2, 2 * S])
        root = sb("root", [P, S])
        rinv = sb("rinv", [P, S])
        V_ = sb("params", [P, NV])
        C_ = sb("consts", [P, NC])
        ones = sb("ones", [P, P])
        eps = sb("eps", [P, 1])
        mhalf = sb("mhalf", [P, 8])
        qscale = sb("qscale", [P, KD])
        ident = C_[:, IDN:IDN + P]
        dist = C_[:, DIST:DIST + 384]

        scratch = sb("scratch", [P, 12800])
        at = 0

        def part(n):
            nonlocal at
            v = scratch[:, at:at + n]
            at += n
            return v

        U = part(KD * (PAD + S)).rearrange("p (c t) -> p c t", c=KD)
        V = part(KD * S).rearrange("p (c t) -> p c t", c=KD)
        SZ = part(2 * KD * S).rearrange("p (c t) -> p c t", c=2 * KD)
        YP = part(KD * S).rearrange("p (c t) -> p c t", c=KD)
        SG = part(2 * S)
        AP = part(2 * (APAD + S)).rearrange("p (c t) -> p c t", c=2)
        W1 = part(2 * (APAD + S)).rearrange("p (c t) -> p c t", c=2)
        W2 = part(2 * (APAD + S)).rearrange("p (c t) -> p c t", c=2)
        FX = part(2 * 15).rearrange("p (c t) -> p c t", c=2)
        assert at <= 12800
        diag = SZ[:, 0:KD, :].rearrange("p c t -> p (c t)").rearrange("p (k m) -> p k m", m=P)
        at = 0
        SZ1 = part(KD * S).rearrange("p (c t) -> p c t", c=KD)
        qT = part(4 * S).rearrange("p (b c t) -> p b c t", b=2, c=2)
        kT = part(4 * S).rearrange("p (b c t) -> p b c t", b=2, c=2)
        vv = part(4 * S).rearrange("p (b t c) -> p b t c", b=2, t=2)
        qn = part(4 * S).rearrange("p (b t c) -> p b t c", b=2, t=2)
        sq1 = part(2 * S)
        neg = part(2 * 384).rearrange("p (b c) -> p b c", b=2)
        prob = part(2 * 384).rearrange("p (b c) -> p b c", b=2)
        pT = part(2 * 384).rearrange("p (b c) -> p b c", b=2)
        oz = part(2 * S).rearrange("p (b c) -> p b c", b=2)
        ss = part(2 * 8).rearrange("p (b c) -> p b c", b=2)
        sr = part(2 * 8).rearrange("p (b c) -> p b c", b=2)
        si = part(2 * 8).rearrange("p (b c) -> p b c", b=2)
        nmax = part(2 * 2).rearrange("p (b c) -> p b c", b=2)
        den = part(2 * 2).rearrange("p (b c) -> p b c", b=2)
        rden = part(2 * 2).rearrange("p (b c) -> p b c", b=2)
        assert at <= 12800

        bank = [ctx.enter_context(nc.psum_tensor(f"bank{i}", [P, 512], F32)) for i in range(8)]
        TR, SC, PV = bank[4], (bank[5], bank[6]), bank[7]

        x_in = [sem(f"x_in{i}") for i in range(2)]
        vec_in, const_in, stored = sem("vec_in"), sem("const_in"), sem("stored")
        raw_in = [sem(f"raw_in{i}") for i in range(RAW)]
        ones_set, pads_set, qs_set = sem("ones_set"), sem("pads_set"), sem("qs_set")
        hi_cut, lo_cut = sem("hi_cut"), sem("lo_cut")
        unit_done = sem("unit_done")
        sq_ready, sq_used = sem("sq_ready"), sem("sq_used")
        rms_sum = sem("rms_sum")
        root_ready, rinv_ready = sem("root_ready"), sem("rinv_ready")
        h_ready, hhi_ready, hlo_ready = sem("h_ready"), sem("hhi_ready"), sem("hlo_ready")
        late = sem("late")
        diag_ready, conv_done, conv_out = sem("diag_ready"), sem("conv_done"), sem("conv_out")
        sig_ready, u_ready = sem("sig_ready"), sem("u_ready")
        a_ready, win, pooled, phi_ready, plo_ready = (
            sem("a_ready"), sem("win"), sem("pooled"), sem("phi_ready"), sem("plo_ready"))
        sz_ready, yp_ready = sem("sz_ready"), sem("yp_ready")
        ya_ready, yahi_ready, yalo_ready = sem("ya_ready"), sem("yahi_ready"), sem("yalo_ready")
        tap = sem("tap")
        mean_sum, centred, normed, swished = sem("mean_sum"), sem("centred"), sem("normed"), sem("swished")
        yb_ready, ybhi_ready, yblo_ready = sem("yb_ready"), sem("ybhi_ready"), sem("yblo_ready")
        bank_closed, x_updated = sem("bank_closed"), sem("x_updated")
        sz1_ready = sem("sz1_ready")
        qk_sq, qk_ss, qk_sr, qk_si, qk_normed = (
            sem("qk_sq"), sem("qk_ss"), sem("qk_sr"), sem("qk_si"), sem("qk_normed"))
        qk_turned, qk_out, v_out = sem("qk_turned"), sem("qk_out"), sem("v_out")
        scored, neg_ready, exped, rden_ready, prob_ready = (
            sem("scored"), sem("neg_ready"), sem("exped"), sem("rden_ready"), sem("prob_ready"))
        p_turned, p_out, pv_done, oz_ready, ozhi_ready, ozlo_ready = (
            sem("p_turned"), sem("p_out"), sem("pv_done"), sem("oz_ready"), sem("ozhi_ready"), sem("ozlo_ready"))

        block = ctx.enter_context(nc.Block())

        def squares(group, m):
            if group == 1 and m >= 2:
                return (W1, W2)[m % 2].rearrange("p c t -> p (c t)")[:, 0:2 * S]
            return SQ[:, m % 2, :]

        def column(c, n=1):
            return V_[:, c:c + n]

        def halves(t, slot, half):
            return t[:, slot, half * (UNIT // 2):(half + 1) * (UNIT // 2)]

        @block.sync
        def _(sp):
            for i in range(2):
                sp.dma_start(X[:, 4 * i:4 * i + 4, :], xT[:, 4 * i:4 * i + 4, :]).then_inc(x_in[i], 16)
            for n in range(NU):
                m = n - RAW
                if m >= 0:
                    if m in NATIVE:
                        sp.wait_ge(unit_done, m + 1)
                    else:
                        sp.wait_ge(lo_cut, 2 * cut_index(m) + 2)
                sp.dma_start(raw[:, n % RAW, :], w[n, :, :]).then_inc(raw_in[n % RAW], 16)
                if n == 3:
                    sp.dma_start(C_[:, :], const).then_inc(const_in, 16)
            for m in range(4):
                sp.wait_ge(x_updated, 4 + m + 1)
                sp.dma_start(out[:, 2 * m:2 * m + 2, :], X[:, 2 * m:2 * m + 2, :]).then_inc(stored, 16)
            sp.wait_ge(stored, 64)

        @block.gpsimd
        def _(pool):
            nc.gpsimd.memset(ones[:, :], 1.0 / D).then_inc(ones_set, 1)
            nc.gpsimd.memset(eps[:, :], EPS).then_inc(ones_set, 1)
            nc.gpsimd.memset(mhalf[:, :], -0.5).then_inc(pads_set, 1)
            nc.gpsimd.memset(U[:, :, 0:PAD], 0.0).then_inc(pads_set, 1)
            nc.gpsimd.memset(AP[:, :, 0:APAD], 0.0).then_inc(pads_set, 1)
            pool.wait_ge(vec_in, 16)
            pool.wait_ge(const_in, 16)
            pool.wait_ge(pads_set, 3)
            nc.gpsimd.tensor_tensor(qscale[:, :], C_[:, QSC:QSC + KD], column(GQ).to_broadcast([P, KD]),
                                    ALU.mult).then_inc(qs_set, 1)
            for a, b in ((0, CONV_CUT), (CONV_CUT, TAPS)):
                pool.wait_ge(qs_set, 1)
                if a:
                    pool.wait_ge(conv_done, 1)
                w0 = CW + TAPS * CONV_PE
                nc.gpsimd.tensor_tensor(diag[:, 0:b - a, :], ident.unsqueeze(1).to_broadcast([P, b - a, P]),
                                        V_[:, w0 + a:w0 + b].unsqueeze(2).to_broadcast([P, b - a, P]),
                                        ALU.mult).then_inc(diag_ready, 1)
            for r in range(8):
                pool.wait_ge(qk_ss, r + 1)
                nc.gpsimd.tensor_scalar(sr[:, r % 2, :], ss[:, r % 2, :], EPS, None, ALU.add).then_inc(qk_sr, 1)
                pool.wait_ge(qk_sr, r + 1)
                nc.gpsimd.tensor_tensor(si[:, r % 2, :], sr[:, r % 2, :], mhalf[:, :], ALU.pow).then_inc(qk_si, 1)

        @block.scalar
        def _(act):
            def cut_hi(n):
                if n >= NU or n in NATIVE:
                    return
                s = cut_index(n)
                act.wait_ge(raw_in[n % RAW], 16 * (n // RAW + 1))
                if s >= CUT:
                    act.wait_ge(unit_done, CUTS[s - CUT] + 1)
                for half in range(2):
                    nc.scalar.copy(halves(w_hi, s % CUT, half), halves(raw, n % RAW, half)).then_inc(hi_cut, 1)

            def square(group, m, source):
                if m >= 2 and group != 1:
                    act.wait_ge(sq_used, 3 * group + m - 1)
                elif m < 2 and group >= 1:
                    act.wait_ge(rms_sum, group)
                nc.scalar.activation(squares(group, m), source[:, 2 * m:2 * m + 2, :], ACT.Square).then_inc(sq_ready, 1)

            def take_root(source, n):
                act.wait_ge(rms_sum, n)
                nc.scalar.activation(root[:, :], source[:, 0:S], ACT.Sqrt, bias=eps[:, 0:1]).then_inc(root_ready, 1)

            def high_h(step, m):
                act.wait_ge(h_ready, 4 * step + m + 1)
                to = h_hi if step % 2 else ya_hi
                nc.scalar.copy(to[:, 2 * m:2 * m + 2, :], H[:, 2 * m:2 * m + 2, :]).then_inc(hhi_ready, 1)

            def late_gate(layer, i, dst, func, done):
                act.wait_ge(late, 2 * layer + i + 1)
                nc.scalar.activation(dst, dst, func).then_inc(done, 1)

            act.dma_start(V_[:, :], vec).then_inc(vec_in, 16)
            for m in range(4):
                high_h(0, m)
            square(0, 0, X)
            square(0, 1, X)
            cut_hi(0)
            cut_hi(1)
            square(0, 2, X)
            square(0, 3, X)
            cut_hi(2)
            act.wait_ge(ones_set, 2)
            take_root(bank[4], 1)
            for m in range(4):
                high_h(1, m)
            late_gate(0, 0, SG[:, :], ACT.Sigmoid, sig_ready)

            for n in range(1, OA[0] + 1):
                cut_hi(n + 2)
                if n - 1 in ZA:
                    i = n - 1 - ZA[0]
                    act.wait_ge(ya_ready, i + 1)
                    nc.scalar.copy(ya_hi[:, 2 * i:2 * i + 2, :], SZ[:, 2 * i:2 * i + 2, :]).then_inc(yahi_ready, 1)
                if n in ZB:
                    g = n - ZB[0]
                    act.wait_ge(pooled, g + 1)
                    nc.scalar.copy(yb_hi[:, 2 * g:2 * g + 2, :], YP[:, 2 * g:2 * g + 2, :]).then_inc(phi_ready, 1)
                if n in BG:
                    i = n // 2
                    act.wait_ge(unit_done, n + 1)
                    if i >= 1:
                        act.wait_ge(u_ready, i)
                    nc.scalar.activation(SG[:, :], bank[n % 4][:, :], ACT.Sigmoid).then_inc(sig_ready, 1)
                if n in A:
                    g = n - A[0]
                    act.wait_ge(unit_done, n + 1)
                    if g == 0:
                        act.wait_ge(pads_set, 3)
                    else:
                        act.wait_ge(pooled, g)
                    nc.scalar.copy(AP[:, :, APAD:APAD + S],
                                   bank[n % 4][:, :].rearrange("p (c t) -> p c t", c=2)).then_inc(a_ready, 1)
                if n in ZB or n in ZA:
                    i = n - ZB[0] if n in ZB else n - ZA[0]
                    c = (KD if n in ZB else 0) + 2 * i
                    act.wait_ge(unit_done, n + 1)
                    nc.scalar.activation(SZ[:, c:c + 2, :], bank[n % 4][:, :].rearrange("p (c t) -> p c t", c=2),
                                         ACT.Silu).then_inc(sz_ready, 1)
                if n == A[3]:
                    act.wait_ge(conv_done, 2)
                    nc.scalar.activation(V[:, CONV_PE, :], bank[5][:, 0:S], ACT.Identity,
                                         bias=column(CB + CONV_PE)).then_inc(conv_out, 1)
                if n == PW:
                    act.wait_ge(unit_done, n + 1)
                    act.wait_ge(plo_ready, 4)
                    for e in range(KD):
                        nc.scalar.mul(YP[:, e, :], bank[4 + e // 2][:, S * (e % 2):S * (e % 2) + S],
                                      column(PS + e)).then_inc(yp_ready, 1)

            cut_hi(OA[0] + 3)
            for m in range(4):
                act.wait_ge(centred, m + 1)
                square(1, m, V)
            cut_hi(OB[0])
            take_root(bank[1], 2)
            for m in range(5):
                for c in (2 * m, 2 * m + 1) if m < 4 else ():
                    act.wait_ge(normed, m + 1)
                    nc.scalar.activation(V[:, c, :], V[:, c, :], ACT.Silu, bias=column(CBETA + c),
                                         scale=column(CG + c)).then_inc(swished, 1)
                if m >= 1:
                    act.wait_ge(yb_ready, m)
                    nc.scalar.copy(yb_hi[:, 2 * m - 2:2 * m, :], SZ[:, KD + 2 * m - 2:KD + 2 * m, :]).then_inc(ybhi_ready, 1)
            for n in range(OB[1], Z1[1]):
                cut_hi(n)

            for m in range(4):
                act.wait_ge(x_updated, m + 1)
                square(2, m, X)
                high_h(2, m)
            cut_hi(Z1[1])
            cut_hi(Z1[2])
            take_root(bank[0], 3)
            for m in range(4):
                high_h(3, m)

            def head_exp(h):
                for t, (a, b) in enumerate(((0, 128), (128, 384))):
                    act.wait_ge(neg_ready, 2 * h + t + 1)
                    if h >= 2 and t == 0:
                        act.wait_ge(p_turned, h - 1)
                    nc.scalar.activation(prob[:, h % 2, a:b], neg[:, h % 2, a:b], ACT.Exp, scale=-1.0,
                                         bias=nmax[:, h % 2, t:t + 1],
                                         accum_out=den[:, h % 2, t:t + 1]).then_inc(exped, 1)

            def head_turn_out(h):
                act.wait_ge(p_turned, h + 1)
                if h >= 2:
                    act.wait_ge(pv_done, h - 1)
                nc.scalar.copy(pT[:, h % 2, :], TR[:, 0:384]).then_inc(p_out, 1)

            def heads_hi(pair):
                act.wait_ge(oz_ready, pair + 1)
                nc.scalar.copy(ya_hi[:, pair, :], oz[:, pair % 2, :]).then_inc(ozhi_ready, 1)

            def attention_step(j, s):
                for quad, at in ((j - 1, s + STEPS), (j, s)):
                    if not 0 <= quad < 4:
                        continue
                    scores, turns, values = head_steps(quad)
                    for i in range(4):
                        if at == scores[i] + 1:
                            head_exp(4 * quad + i)
                        if at == turns[i]:
                            head_turn_out(4 * quad + i)
                    for i in (1, 3):
                        if at == values[i] + 2:
                            heads_hi(2 * quad + i // 2)

            for i, n in enumerate(Z1):
                if i:
                    cut_hi(n + 2)
                to = SZ1[:, 2 * i:2 * i + 2, :]
                if n in EARLY[1]:
                    late_gate(1, i, to, ACT.Silu, sz1_ready)
                else:
                    act.wait_ge(unit_done, n + 1)
                    nc.scalar.activation(to, bank[n % 4][:, :].rearrange("p (c t) -> p c t", c=2),
                                         ACT.Silu).then_inc(sz1_ready, 1)

            def qk_squares(n, j, isq):
                r = 2 * j + isq
                act.wait_ge(unit_done, n + 1)
                if r >= 1:
                    act.wait_ge(qk_ss, r)
                nc.scalar.activation(sq1[:, :], bank[n % 4][:, :], ACT.Square, scale=DH ** -0.5).then_inc(qk_sq, 1)

            def qk_turn_out(j, isq):
                r = 2 * j + isq
                act.wait_ge(qk_turned, r + 1)
                if isq:
                    act.wait_ge(qs_set, 1)
                for c in range(2):
                    nc.scalar.mul((qT if isq else kT)[:, j % 2, c, :], TR[:, c * S:c * S + S],
                                  qscale[:, 2 * j + c:2 * j + c + 1] if isq else column(GK)).then_inc(qk_out, 1)

            for j in range(4):
                for u, n in enumerate((KU[j], QU[j], VU[j])):
                    for step in range(8):
                        s = 8 * u + step
                        if j and s == QT_AT - STEPS:
                            qk_turn_out(j - 1, 1)
                        attention_step(j - 1, s)
                        if step == CUT_HI_AT:
                            cut_hi(n + 2)
                        if s == KT_AT:
                            qk_turn_out(j, 0)
                    if u < 2:
                        qk_squares(n, j, u)
                    else:
                        act.wait_ge(unit_done, n + 1)
                        if j >= 2:
                            act.wait_ge(pv_done, 4 * (j - 1))
                        nc.scalar.copy(vv[:, j % 2, :, :], bank[n % 4][:, :].rearrange("p (t c) -> p t c", t=2)
                                       ).then_inc(v_out, 1)
            for s in range(STEPS + 12):
                if s == QT_AT - STEPS:
                    qk_turn_out(3, 1)
                attention_step(3 + s // STEPS, s % STEPS)
                if s == 2:
                    cut_hi(O1[0] + 2)
                if s == 10:
                    cut_hi(O1[0] + 3)

        @block.vector
        def _(dve):
            def cut_lo(n):
                if n >= NU or n in NATIVE:
                    return
                s = cut_index(n)
                for half in range(2):
                    dve.wait_ge(hi_cut, 2 * s + half + 1)
                    nc.vector.tensor_tensor(halves(w_lo, s % CUT, half), halves(raw, n % RAW, half),
                                            halves(w_hi, s % CUT, half).bitcast(F32), ALU.subtract).then_inc(lo_cut, 1)

            def gained(layer, m):
                for c in (2 * m, 2 * m + 1):
                    last = nc.vector.tensor_scalar(H[:, c, :], X[:, c, :], column((G0, G1)[layer] + c), None, ALU.mult)
                last.then_inc(h_ready, 1)

            def low_h(step, m):
                dve.wait_ge(hhi_ready, 4 * step + m + 1)
                hi, lo = (h_hi, h_lo) if step % 2 else (ya_hi, ya_lo)
                nc.vector.tensor_tensor(lo[:, 2 * m:2 * m + 2, :], H[:, 2 * m:2 * m + 2, :],
                                        hi[:, 2 * m:2 * m + 2, :].bitcast(F32), ALU.subtract).then_inc(hlo_ready, 1)

            def take_inverse(n):
                dve.wait_ge(root_ready, n)
                nc.vector.reciprocal(rinv[:, :], root[:, :]).then_inc(rinv_ready, 1)
                dve.wait_ge(rinv_ready, n)

            def over_rms(layer):
                for m in range(5):
                    if m < 4:
                        nc.vector.tensor_tensor(H[:, 2 * m:2 * m + 2, :], H[:, 2 * m:2 * m + 2, :],
                                                rinv[:, :].unsqueeze(1).to_broadcast([P, 2, S]),
                                                ALU.mult).then_inc(h_ready, 1)
                    if m:
                        low_h(2 * layer + 1, m - 1)

            def scale_late(layer, i, dst):
                n = EARLY[layer][i]
                dve.wait_ge(unit_done, n + 1)
                nc.vector.tensor_tensor(dst, bank[n % 4][:, :].rearrange("p (c t) -> p c t", c=2),
                                        rinv[:, :].unsqueeze(1).to_broadcast([P, 2, S]), ALU.mult).then_inc(late, 1)

            SG2 = SG[:, :].rearrange("p (c t) -> p c t", c=2)
            dve.wait_ge(vec_in, 16)
            for m in range(5):
                if m < 4:
                    if m % 2 == 0:
                        dve.wait_ge(x_in[m // 2], 16)
                    gained(0, m)
                if m:
                    low_h(0, m - 1)
            cut_lo(0)
            cut_lo(1)
            cut_lo(2)
            take_inverse(1)
            over_rms(0)
            scale_late(0, 0, SG2)

            def window_sums(g):
                width = WINDOWS[g]
                dve.wait_ge(a_ready, g + 1)
                src = AP
                count = sum(lv + 2 for lv in range(g))
                for lv in range(g + 1):
                    shift = 1 << lv
                    lo = APAD if lv == g else 2 * shift
                    dst = (W1, W2)[lv % 2]
                    if lv:
                        dve.wait_ge(win, count + lv)
                    nc.vector.tensor_tensor(dst[:, :, lo:APAD + S], src[:, :, lo:APAD + S],
                                            src[:, :, lo - shift:APAD + S - shift], ALU.add).then_inc(win, 1)
                    src = dst
                dve.wait_ge(win, count + g + 1)
                F = width - 1
                inv = C_[:, IC + 15 * g:IC + 15 * g + F].unsqueeze(1).to_broadcast([P, 2, F])
                nc.vector.scalar_tensor_tensor(YP[:, 2 * g:2 * g + 2, F:S], src[:, :, APAD + F:APAD + S], 1.0 / width,
                                               AP[:, :, APAD + F:APAD + S], ALU.mult, ALU.subtract)
                if g == 0:
                    dve.wait_ge(const_in, 16)
                nc.vector.tensor_tensor(FX[:, :, 0:F], src[:, :, APAD:APAD + F], inv, ALU.mult).then_inc(win, 1)
                dve.wait_ge(win, count + g + 2)
                nc.vector.tensor_tensor(YP[:, 2 * g:2 * g + 2, 0:F], FX[:, :, 0:F], AP[:, :, APAD:APAD + F],
                                        ALU.subtract).then_inc(pooled, 1)

            done = 0

            def taps(count, ready):
                nonlocal done
                for _ in range(count):
                    if done == len(CONV_ORDER):
                        return
                    c, k = CONV_ORDER[done]
                    group = next(g for g in CONV_GROUPS if c in g)
                    if max(group) // 2 >= ready:
                        return
                    src = U[:, c, k:k + S]
                    wk = column(CW + TAPS * c + k)
                    if k == 0:
                        if c == group[0]:
                            dve.wait_ge(u_ready, max(group) // 2 + 1)
                        nc.vector.tensor_scalar(V[:, c, :], src, wk, column(CB + c), ALU.mult, ALU.add).then_inc(tap, 1)
                    else:
                        dve.wait_ge(tap, done - len(group) + 1)
                        nc.vector.scalar_tensor_tensor(V[:, c, :], src, wk, V[:, c, :],
                                                       ALU.mult, ALU.add).then_inc(tap, 1)
                    done += 1

            dve.wait_ge(pads_set, 3)
            for n in range(1, OA[0] + 1):
                cut_lo(n + 2)
                m = n - 1
                if m in BV:
                    i = m // 2
                    dve.wait_ge(sig_ready, i + 1)
                    dve.wait_ge(unit_done, m + 1)
                    value = bank[m % 4][:, :].rearrange("p (c t) -> p c t", c=2)
                    if m in EARLY[0]:
                        scale_late(0, 1, W1[:, :, 0:S])
                        dve.wait_ge(late, 2)
                        value = W1[:, :, 0:S]
                    nc.vector.tensor_tensor(U[:, 2 * i:2 * i + 2, PAD:PAD + S], value, SG2, ALU.mult).then_inc(u_ready, 1)
                if m in A:
                    window_sums(m - A[0])
                if n in ZB:
                    g = n - ZB[0]
                    dve.wait_ge(phi_ready, g + 1)
                    nc.vector.tensor_tensor(yb_lo[:, 2 * g:2 * g + 2, :], YP[:, 2 * g:2 * g + 2, :],
                                            yb_hi[:, 2 * g:2 * g + 2, :].bitcast(F32), ALU.subtract).then_inc(plo_ready, 1)
                if m in ZA:
                    i = m - ZA[0]
                    dve.wait_ge(sz_ready, 4 + i + 1)
                    dve.wait_ge(yp_ready, 2 * i + 2)
                    nc.vector.tensor_tensor(SZ[:, 2 * i:2 * i + 2, :], SZ[:, 2 * i:2 * i + 2, :],
                                            YP[:, 2 * i:2 * i + 2, :], ALU.mult).then_inc(ya_ready, 1)
                taps(TAPS_PER_SLOT, (m + 1) // 2)
                if m in ZA:
                    dve.wait_ge(yahi_ready, i + 1)
                    nc.vector.tensor_tensor(ya_lo[:, 2 * i:2 * i + 2, :], SZ[:, 2 * i:2 * i + 2, :],
                                            ya_hi[:, 2 * i:2 * i + 2, :].bitcast(F32), ALU.subtract).then_inc(yalo_ready, 1)
            cut_lo(OA[0] + 3)
            taps(len(CONV_ORDER), 4)

            dve.wait_ge(mean_sum, 1)
            for m in range(4):
                nc.vector.tensor_tensor(V[:, 2 * m:2 * m + 2, :], V[:, 2 * m:2 * m + 2, :],
                                        bank[0][:, 0:S].unsqueeze(1).to_broadcast([P, 2, S]),
                                        ALU.subtract).then_inc(centred, 1)
            cut_lo(OB[0])
            take_inverse(2)
            dve.wait_ge(sq_ready, 8)
            for m in range(4):
                nc.vector.tensor_tensor(V[:, 2 * m:2 * m + 2, :], V[:, 2 * m:2 * m + 2, :],
                                        rinv[:, :].unsqueeze(1).to_broadcast([P, 2, S]), ALU.mult).then_inc(normed, 1)
            dve.wait_ge(sz_ready, 8)
            for m in range(5):
                if m < 4:
                    dve.wait_ge(swished, 2 * m + 2)
                    nc.vector.tensor_tensor(SZ[:, KD + 2 * m:KD + 2 * m + 2, :], SZ[:, KD + 2 * m:KD + 2 * m + 2, :],
                                            V[:, 2 * m:2 * m + 2, :], ALU.mult).then_inc(yb_ready, 1)
                if m >= 1:
                    dve.wait_ge(ybhi_ready, m)
                    nc.vector.tensor_tensor(yb_lo[:, 2 * m - 2:2 * m, :], SZ[:, KD + 2 * m - 2:KD + 2 * m, :],
                                            yb_hi[:, 2 * m - 2:2 * m, :].bitcast(F32), ALU.subtract).then_inc(yblo_ready, 1)
            for n in range(OB[1], Z1[1]):
                cut_lo(n)

            def residual(m, layer):
                if m < 3:
                    dve.wait_ge(bank_closed, 3 * layer + m + 1)
                else:
                    dve.wait_ge(unit_done, (Z1[0], NU)[layer])
                nc.vector.tensor_tensor(X[:, 2 * m:2 * m + 2, :], X[:, 2 * m:2 * m + 2, :],
                                        bank[(4, 0)[layer] + m][:, :].rearrange("p (c t) -> p c t", c=2),
                                        ALU.add).then_inc(x_updated, 1)

            for m in range(5):
                if m < 4:
                    residual(m, 0)
                    dve.wait_ge(x_updated, m + 1)
                    gained(1, m)
                if m:
                    low_h(2, m - 1)
            cut_lo(Z1[1])
            cut_lo(Z1[2])
            take_inverse(3)
            over_rms(1)

            def head_bias(h):
                slope = 2.0 ** (-8.0 * (h + 1) / HEADS)
                dve.wait_ge(scored, h + 1)
                if h >= 2:
                    dve.wait_ge(exped, 2 * h - 2)
                for t, (a, b) in enumerate(((0, 128), (128, 384))):
                    nc.vector.tensor_tensor_reduce(neg[:, h % 2, a:b], dist[:, a:b], SC[h % 2][:, a:b], slope, 3.0e38,
                                                   ALU.add, ALU.min,
                                                   nmax[:, h % 2, t:t + 1]).then_inc(neg_ready, 1)

            def head_scale(h):
                dve.wait_ge(exped, 2 * h + 2)
                nc.vector.reciprocal(rden[:, h % 2, :], den[:, h % 2, :]).then_inc(rden_ready, 1)
                dve.wait_ge(rden_ready, h + 1)
                for t, (a, b) in enumerate(((0, 128), (128, 384))):
                    nc.vector.tensor_scalar(prob[:, h % 2, a:b], prob[:, h % 2, a:b], rden[:, h % 2, t:t + 1], None,
                                            ALU.mult).then_inc(prob_ready, 1)

            def heads_gate(pair):
                dve.wait_ge(pv_done, 2 * pair + 2)
                if pair >= 2:
                    dve.wait_ge(ozlo_ready, pair - 1)
                    dve.wait_ge(ozhi_ready, pair - 1)
                if pair == 0:
                    dve.wait_ge(sz1_ready, 4)
                nc.vector.tensor_tensor(oz[:, pair % 2, :], PV[:, 0:S], SZ1[:, pair, :], ALU.mult).then_inc(oz_ready, 1)

            def heads_lo(pair):
                dve.wait_ge(ozhi_ready, pair + 1)
                nc.vector.tensor_tensor(ya_lo[:, pair, :], oz[:, pair % 2, :], ya_hi[:, pair, :].bitcast(F32),
                                        ALU.subtract).then_inc(ozlo_ready, 1)

            def attention_step(j, s):
                for quad, at in ((j - 1, s + STEPS), (j, s)):
                    if not 0 <= quad < 4:
                        continue
                    scores, turns, values = head_steps(quad)
                    for i in range(4):
                        if at == scores[i]:
                            head_bias(4 * quad + i)
                        if at == scores[i] + 3:
                            head_scale(4 * quad + i)
                    for i in (1, 3):
                        if at == values[i] + 1:
                            heads_gate(2 * quad + i // 2)
                        if at == values[i] + 3:
                            heads_lo(2 * quad + i // 2)

            for i, n in enumerate(Z1):
                if i:
                    cut_lo(n + 2)
                if n in EARLY[1]:
                    scale_late(1, i, SZ1[:, 2 * i:2 * i + 2, :])

            def qk_sums(j, isq):
                r = 2 * j + isq
                dve.wait_ge(qk_sq, r + 1)
                nc.vector.tensor_reduce(ss[:, isq, :], sq1[:, :].rearrange("p (h d) -> p h d", d=DH),
                                        AX_X, ALU.add).then_inc(qk_ss, 1)

            def qk_norm(n, j, isq):
                r = 2 * j + isq
                src = bank[n % 4][:, :].rearrange("p (h d) -> p h d", d=DH)
                dve.wait_ge(qk_si, r + 1)
                if r >= 2:
                    dve.wait_ge(qk_turned, r - 1)
                nc.vector.tensor_tensor(qn[:, isq, :, :].rearrange("p t (h d) -> p (t h) d", d=DH), src,
                                        si[:, isq, :].unsqueeze(2).to_broadcast([P, 8, DH]),
                                        ALU.mult).then_inc(qk_normed, 1)

            for j in range(4):
                for u, n in enumerate((KU[j], QU[j], VU[j])):
                    for step in range(8):
                        attention_step(j - 1, 8 * u + step)
                        if step == SUM_AT and u > 0:
                            qk_sums(j, u - 1)
                        if step == NORM_AT and u > 0:
                            qk_norm(n - 1, j, u - 1)
                        if step == CUT_LO_AT:
                            cut_lo(n + 2)
            for s in range(STEPS + 12):
                attention_step(3 + s // STEPS, s % STEPS)
                if s == 2:
                    cut_lo(O1[0] + 2)
                if s == 10:
                    cut_lo(O1[0] + 3)
            for m in range(4):
                residual(m, 1)

        @block.tensor
        def _(pe):
            def product(dst, stationary, moving, start, stop):
                (wh, wl), (ah, al) = stationary, moving
                nc.tensor.matmul(dst, wh, ah, start=start, stop=False, skip_group_check=True)
                nc.tensor.matmul(dst, wh, al, start=False, stop=False, skip_group_check=True)
                return nc.tensor.matmul(dst, wl, ah, start=False, stop=stop, skip_group_check=True)

            def arrived(n, half):
                if n in NATIVE:
                    if half == 0:
                        pe.wait_ge(raw_in[n % RAW], 16 * (n // RAW + 1))
                else:
                    pe.wait_ge(lo_cut, 2 * cut_index(n) + half + 1)

            def piece(n, a, b):
                s = cut_index(n) % CUT
                return raw[:, n % RAW, a:b], (w_hi[:, s, a:b], w_lo[:, s, a:b])

            def channel_step(n, k, h_wait=None):
                if k % 4 == 0:
                    arrived(n, k // 4)
                if h_wait is not None and k % 2 == 0:
                    pe.wait_ge(hlo_ready, 4 * h_wait + k // 2 + 1)
                hi, lo = (ya_hi, ya_lo) if n in EARLY[0] + EARLY[1] else (h_hi, h_lo)
                for c in range(2):
                    a = k * UC + c * P
                    wr, wp = piece(n, a, a + P)
                    dst = bank[n % 4][:, c * S:c * S + S]
                    start, stop = k == 0 and c == 0, k == KD - 1
                    if n in NATIVE:
                        last = nc.tensor.matmul(dst, wr, H[:, k, :], start=start, stop=stop, skip_group_check=True)
                    else:
                        last = product(dst, wp, (hi[:, k, :], lo[:, k, :]), start, stop)
                if k == KD - 1:
                    last.then_inc(unit_done, 1)

            def token_step(n, k):
                if k % 4 == 0:
                    arrived(n, k // 4)
                _, (wh, wl) = piece(n, k * UC, (k + 1) * UC)
                for t in range(TT):
                    ah, al = h_hi[:, k, t * P:t * P + P], h_lo[:, k, t * P:t * P + P]
                    last = product(bank[n % 4][:, t * UC:t * UC + UC], (ah, al), (wh, wl),
                                   k == 0 and t == 0, k == KD - 1)
                if k == KD - 1:
                    last.then_inc(unit_done, 1)

            def out_product(n, kt, m, y, tile, acc, start, stop):
                a = kt * D + m * P
                wr, wp = piece(n, a, a + P)
                y_hi, y_lo = y
                return product(bank[acc + m // 2][:, S * (m % 2):S * (m % 2) + S], wp,
                               (y_hi[:, tile, :], y_lo[:, tile, :]), start and m % 2 == 0, stop)

            pe.wait_ge(ones_set, 1)
            for _ in range(WARM):
                nc.tensor.matmul(bank[7][:, 0:P], ones[:, :], ones[:, :], start=True, stop=True, skip_group_check=True)

            def square_sums(group, m, dst):
                pe.wait_ge(sq_ready, 4 * group + m + 1)
                nc.tensor.matmul(dst[:, 0:S], ones[:, :], squares(group, m)[:, 0:S], start=(m == 0), stop=False,
                                 skip_group_check=True)
                nc.tensor.matmul(dst[:, 0:S], ones[:, :], squares(group, m)[:, S:2 * S], start=False, stop=(m == 3),
                                 skip_group_check=True).then_inc(rms_sum if m == 3 else sq_used, 1)

            def conv_taps(a, b):
                if a == 0:
                    pe.wait_ge(u_ready, CONV_PE // 2 + 1)
                pe.wait_ge(diag_ready, 1 if a == 0 else 2)
                for k in range(a, b):
                    last = nc.tensor.matmul(bank[5][:, 0:S], diag[:, k - a, :], U[:, CONV_PE, k:k + S],
                                            start=(k == 0), stop=(k == TAPS - 1), skip_group_check=True)
                last.then_inc(conv_done, 1)

            for n in range(PW):
                if n >= 4:
                    m = n - 4
                    if m in BG and m not in EARLY[0]:
                        pe.wait_ge(sig_ready, m // 2 + 1)
                    elif m in BG:
                        pe.wait_ge(late, 1)
                    elif m in BV:
                        pe.wait_ge(u_ready, m // 2 + 1)
                    elif m in A:
                        pe.wait_ge(a_ready, m - A[0] + 1)
                for k in range(KD):
                    channel_step(n, k, {0: 0, 2: 1}.get(n))
                    if n == 0 and k >= 4:
                        square_sums(0, k - 4, bank[4])
                if n in (A[0], A[2]):
                    conv_taps(*((0, CONV_CUT) if n == A[0] else (CONV_CUT, TAPS)))

            n = PW
            for g in range(4):
                if g % 2 == 0:
                    arrived(n, g // 2)
                pe.wait_ge(plo_ready, g + 1)
                if g == 0:
                    pe.wait_ge(root_ready, 1)
                    pe.wait_ge(conv_out, 1)
                for ct in range(2):
                    for e in range(2):
                        a = (2 * g + ct) * UC + e * P
                        wr, wp = piece(n, a, a + P)
                        last = product(bank[4 + g][:, e * S:e * S + S], wp,
                                       (yb_hi[:, 2 * g + ct, :], yb_lo[:, 2 * g + ct, :]), ct == 0 and e == 0, ct == 1)
            last.then_inc(unit_done, 1)

            for n in ZA:
                if n != ZA[3]:
                    pe.wait_ge(sz_ready, n - ZA[0] + 2)
                for k in range(KD):
                    channel_step(n, k)

            def channel_mean(tiles):
                for c in tiles:
                    if c == CONV_PE:
                        pe.wait_ge(conv_out, 1)
                    else:
                        group = next(g for g in CONV_GROUPS if c in g)
                        pe.wait_ge(tap, CONV_ORDER.index((group[-1], TAPS - 1)) + 1)
                    last = nc.tensor.matmul(bank[0][:, 0:S], ones[:, :], V[:, c, :], start=(c == CONV_PE), stop=(c == 6),
                                            skip_group_check=True)
                if tiles[-1] == 6:
                    last.then_inc(mean_sum, 1)

            pe.wait_ge(yp_ready, KD)
            for i, n in enumerate(OA):
                pe.wait_ge(yalo_ready, i + 1)
                for kt in range(2):
                    arrived(n, kt)
                    for m in range(KD):
                        last = out_product(n, kt, m, (ya_hi, ya_lo), 2 * i + kt, 4, i == 0 and kt == 0, False)
                    if i == 2 and kt == 0:
                        for m in range(4):
                            square_sums(1, m, bank[1])
                last.then_inc(unit_done, 1)
                if i == 0:
                    pe.wait_ge(sz_ready, 8)
                    channel_mean((CONV_PE, 0, 1, 2, 3))
                if i == 1:
                    channel_mean((4, 5, 6))

            for i in range(2):
                n = OB[i]
                pe.wait_ge(yblo_ready, i + 1)
                for kt in range(2):
                    arrived(n, kt)
                    for m in range(KD):
                        last = out_product(n, kt, m, (yb_hi, yb_lo), 2 * i + kt, 4, False, False)
                last.then_inc(unit_done, 1)

            def closing(units, y, first_tile, acc, ready, sums=False):
                pe.wait_ge(ready[0], ready[1])
                for n in units:
                    arrived(n, 1)
                for m in range(KD):
                    for u, n in enumerate(units):
                        for kt in range(2):
                            last = out_product(n, kt, m, y, first_tile + 2 * u + kt, acc, False, u == len(units) - 1 and kt == 1)
                        if m == KD - 1 and u == 0 and len(units) == 2:
                            last.then_inc(unit_done, 1)
                    if m % 2 == 1 and m < KD - 1:
                        last.then_inc(bank_closed, 1)
                    if m in (4, 6) and sums:
                        square_sums(2, m // 2 - 2, bank[0])
                last.then_inc(unit_done, 1)

            closing(OB[2:], (yb_hi, yb_lo), 4, 4, (yblo_ready, 4), sums=True)

            for n in Z1:
                if n % 4 == 0:
                    pe.wait_ge(root_ready, 3)
                for k in range(KD):
                    channel_step(n, k, {Z1[0]: 2, Z1[2]: 3}.get(n))
                    if n == Z1[0] and k in (1, 6):
                        square_sums(2, 2 if k == 1 else 3, bank[0])

            def turn_qk(j, isq):
                pe.wait_ge(qk_normed, 2 * j + isq + 1)
                turn_bank_free()
                for c in range(2):
                    for t in range(TT):
                        last = nc.tensor.transpose(TR[:, c * S + t * P:c * S + t * P + P],
                                                   qn[:, isq, t, c * P:c * P + P], ident)
                last.then_inc(qk_turned, 1)
                turned.append(("qk", 4 * j + 2 * isq + 2))

            turned = []

            def turn_bank_free():
                if turned:
                    kind, count = turned[-1]
                    pe.wait_ge(qk_out if kind == "qk" else p_out, count)

            def head_scores(h):
                j, c, r = h // 4, (h // 2) % 2, DH * (h % 2)
                pe.wait_ge(qk_out, 4 * j + 4)
                if h >= 2:
                    pe.wait_ge(neg_ready, 2 * h - 2)
                nc.tensor.matmul(SC[h % 2][:, 0:P], qT[r:r + DH, j % 2, c, 0:P], kT[r:r + DH, j % 2, c, 0:P],
                                 start=True, stop=True, skip_group_check=True)
                nc.tensor.matmul(SC[h % 2][:, P:P + S], qT[r:r + DH, j % 2, c, P:S], kT[r:r + DH, j % 2, c, :],
                                 start=False, stop=True, skip_group_check=True).then_inc(scored, 1)

            def head_turn(h):
                pe.wait_ge(prob_ready, 2 * h + 2)
                turn_bank_free()
                for i, (a, b) in enumerate(((0, 0), (128, 128), (256, 256))):
                    last = nc.tensor.transpose(TR[:, a:a + P], prob[:, h % 2, b:b + P], ident)
                last.then_inc(p_turned, 1)
                turned.append(("p", h + 1))

            def head_values(h):
                j, r = h // 4, DH * (h % 2)
                pe.wait_ge(p_out, h + 1)
                pe.wait_ge(v_out, j + 1)
                if h % 2 == 0 and h >= 2:
                    pe.wait_ge(oz_ready, h // 2)
                a = DH * (h % 4)
                nc.tensor.matmul(PV[r:r + DH, 0:S], vv[:, j % 2, 0, a:a + DH], pT[:, h % 2, 0:S],
                                 start=True, stop=False, skip_group_check=True)
                nc.tensor.matmul(PV[r:r + DH, P:S], vv[:, j % 2, 1, a:a + DH], pT[:, h % 2, S:S + P],
                                 start=False, stop=True, skip_group_check=True).then_inc(pv_done, 1)

            def attention_step(j, s):
                for quad, at in ((j - 1, s + STEPS), (j, s)):
                    if not 0 <= quad < 4:
                        continue
                    scores, turns, values = head_steps(quad)
                    for i in range(4):
                        if at == scores[i]:
                            head_scores(4 * quad + i)
                        if at == turns[i]:
                            head_turn(4 * quad + i)
                        if at == values[i]:
                            head_values(4 * quad + i)

            pe.wait_ge(const_in, 16)
            for j in range(4):
                for u, n in enumerate((KU[j], QU[j], VU[j])):
                    m = n - 4
                    if m in Z1:
                        pe.wait_ge(sz1_ready, m - Z1[0] + 1)
                    elif m in VU:
                        pe.wait_ge(v_out, VU.index(m) + 1)
                    else:
                        pe.wait_ge(qk_normed, 2 * ((m - KU[0]) // 3) + (m - KU[0]) % 3 + 1)
                    for k in range(KD):
                        s = 8 * u + k
                        if s == KT_AT:
                            turn_qk(j, 0)
                        if j and s == QT_AT - STEPS:
                            turn_qk(j - 1, 1)
                        attention_step(j - 1, s)
                        token_step(n, k)

            pe.wait_ge(qk_normed, 8)
            s = 0
            for i in range(3):
                n = O1[i]
                for kt in range(2):
                    pe.wait_ge(ozlo_ready, 2 * i + kt + 1)
                    arrived(n, kt)
                    for m in [2, 3, 4, 5, 6, 7, 0, 1]:
                        if m % 2 == 0:
                            if s == QT_AT - STEPS:
                                turn_qk(3, 1)
                            attention_step(3, s)
                            s += 1
                        if i == 0 and kt == 0 and m == 0:
                            pe.wait_ge(v_out, 4)
                        last = out_product(n, kt, m, (ya_hi, ya_lo), 2 * i + kt, 0, i == 0 and kt == 0, False)
                last.then_inc(unit_done, 1)
            while s < STEPS + 12:
                attention_step(4, s % STEPS)
                s += 1
            pe.wait_ge(ozlo_ready, 7)
            arrived(O1[3], 0)
            for m in range(KD):
                out_product(O1[3], 0, m, (ya_hi, ya_lo), 6, 0, False, False)
            pe.wait_ge(ozlo_ready, 8)
            arrived(O1[3], 1)
            for m in range(KD):
                last = out_product(O1[3], 1, m, (ya_hi, ya_lo), 7, 0, False, True)
                if m % 2 == 1:
                    last.then_inc(bank_closed if m < KD - 1 else unit_done, 1)


def kernel(x, norm0_g, w_in0, pool_w, pool_scale, conv_w, conv_b, cnorm_g, cnorm_b, w_out0,
           norm1_g, w_in1, q_norm_g, k_norm_g, w_out1):
    import numpy as np
    import concourse.bacc as bacc
    from concourse.bass_utils import run_bass_kernel_spmd

    def tiles(v):
        return np.asarray(v).reshape(KD, P).T

    def columns(wt, c):
        return np.asarray(wt)[0][:, c:c + UC].reshape(KD, P, UC).transpose(1, 0, 2).reshape(P, UNIT)

    def rows(wt, i):
        return np.asarray(wt)[0][2 * P * i:2 * P * (i + 1)].reshape(2, P, D).transpose(1, 0, 2).reshape(P, UNIT)

    units = []
    for i in range(4):
        units += [columns(w_in0, 2 * D + UC * i), columns(w_in0, D + UC * i)]
    units += [columns(w_in0, UC * g) for g in range(4)]
    units += [columns(w_in0, 4 * D + UC * i) for i in range(4)]
    units += [np.asarray(pool_w)[0].reshape(4, 2, P, UC).transpose(2, 0, 1, 3).reshape(P, UNIT)]
    units += [columns(w_in0, 3 * D + UC * i) for i in range(4)]
    units += [rows(w_out0, i) for i in range(8)]
    units += [columns(w_in1, 3 * D + UC * i) for i in range(4)]
    for j in range(4):
        units += [columns(w_in1, D + UC * j), columns(w_in1, UC * j), columns(w_in1, 2 * D + UC * j)]
    units += [rows(w_out1, i) for i in range(4)]
    taps = np.asarray(conv_w)[0].reshape(TAPS, KD, P).transpose(2, 1, 0).reshape(P, KD * TAPS)
    twice = [np.concatenate([np.asarray(g)[0]] * 2)[:, None] for g in (q_norm_g, k_norm_g)]
    vec = np.concatenate([tiles(norm0_g), tiles(pool_scale), tiles(conv_b), tiles(cnorm_g), tiles(cnorm_b),
                          tiles(norm1_g)] + twice + [taps], axis=1)
    t = np.arange(15)
    inv = np.concatenate([1.0 / np.minimum(t + 1, wd) for wd in WINDOWS])
    q, k = np.arange(P)[:, None], np.arange(P)[None, :]
    own = np.where(q >= k, q - k, FAR)
    heads = 2 * np.arange(KD)[None, :] + np.arange(P)[:, None] // DH
    scale = -DH ** -0.5 * 2.0 ** (8.0 * (heads + 1) / HEADS)
    const = np.concatenate([np.broadcast_to(inv, (P, 60)), own, q - k + P, own, np.eye(P), scale], axis=1).astype(np.float32)
    arrays = {
        "xT": np.ascontiguousarray(np.asarray(x)[0].T.reshape(KD, P, S).transpose(1, 0, 2)),
        "w": np.ascontiguousarray(np.stack(units)),
        "vec": np.ascontiguousarray(vec),
        "const": const,
    }
    nc = bacc.Bacc("TRN2", target_bir_lowering=False, num_devices=1)
    args = [nc.dram_tensor(n, a.shape, F32, kind="ExternalInput").ap() for n, a in arrays.items()]
    out = nc.dram_tensor("out", (P, KD, S), F32, kind="ExternalOutput").ap()
    hybrid_trunk(nc, *args, out)
    r = run_bass_kernel_spmd(nc, [arrays], core_ids=[0])
    return r.results[0]["out"].transpose(1, 0, 2).reshape(D, S).T[None]
```

```python
from contextlib import ExitStack

import concourse.bass as bass
from concourse import mybir

F32 = mybir.dt.float32
F32R = mybir.dt.float32r
ALU = mybir.AluOpType
ACT = mybir.ActivationFunctionType
AX_X = mybir.AxisListType.X

P = 128
S = 256
D = 1024
KD = D // P
TT = S // P
HEADS, DH = 16, 64
TAPS = 31
PAD = TAPS - 1
EPS = 1e-6
UNIT = 2048
UC = UNIT // KD
WINDOWS = (2, 4, 8, 16)
APAD = 16
FAR = 1.0e30

BG = [2 * i for i in range(4)]
BV = [2 * i + 1 for i in range(4)]
A = [8 + g for g in range(4)]
ZB = [12 + i for i in range(4)]
PW = 16
ZA = [17 + i for i in range(4)]
OA = [21 + i for i in range(4)]
OB = [25 + i for i in range(4)]
Z1 = [29 + i for i in range(4)]
KU = [33 + 3 * j for j in range(4)]
QU = [34 + 3 * j for j in range(4)]
VU = [35 + 3 * j for j in range(4)]
O1 = [45 + i for i in range(4)]
NU = 49

NATIVE = frozenset((0, 5, 7, 9, 11, 13, 15, 17, 21, 22, 25))
WARM = 20
RAW = 4
CUT = 3

G0, PS, CB, CG, CBETA, G1 = (8 * i for i in range(6))
GQ, GK = 48, 49
CW = 50
NV = CW + KD * TAPS
IC = 0
DIST = IC + 4 * 15
IDN = DIST + 384
QSC = IDN + P
NC = QSC + KD


def cut_index(n):
    return sum(1 for m in range(n) if m not in NATIVE)


CUTS = [n for n in range(NU) if n not in NATIVE]


def pairs_cut(units, i):
    return sum(1 for n in units[:i] if n not in NATIVE)

STEPS = 24
CUT_HI_AT, CUT_LO_AT = 2, 5
SUM_AT, NORM_AT = 0, 4
KT_AT, QT_AT = 15, STEPS + 1


def head_steps(j):
    gap, to_turn, to_values, first = (6, 7, 10, 4) if j < 3 else (4, 6, 9, 3)
    scores = [gap * i + first for i in range(4)]
    return scores, [s + to_turn for s in scores], [s + to_values for s in scores]



CONV_GROUPS = ((0, 1), (2, 3), (4, 5), (6,))
CONV_PE = 7
CONV_CUT = 16
BUILD = range(2, 8)
PER_BUILD = 6
LEAD = 6
PRODUCTS = 4
LAST_PRODUCT = ZA[0] - 1


def conv_order():
    first = [(g, k) for g in (0, 2) for k in range(1, TAPS)]
    second = [(g, k) for g in (1, 3) for k in range(1, TAPS)]
    order = first[:LEAD]
    for i in range(len(second)):
        order += [second[i]] + first[LEAD + i:LEAD + i + 1]
    return order


def conv_plan():
    plan, last, used, count, rest = {}, {}, [], 0, conv_order()
    for n in range(BV[1], OA[0] + 1):
        plan[n] = []
        budget = LONG_SLOT if n in (A[2] + 1, ZB[0] + 1) else SLOT
        while rest and (budget > 0 or n == OA[0]):
            g, k = rest[0]
            tiles = CONV_GROUPS[g]
            pair = tiles[0] // 2
            if pair >= n // 2:
                break
            rest.pop(0)
            if len(tiles) == 2 and k in PRODUCT_TAPS and pair < (n - 1) // 2 and A[0] - 3 <= n <= LAST_PRODUCT:
                count += 1
                plan[n].append((tiles, k, len(used), max(last.get(c, 0) for c in tiles), count))
                used.append(count)
                budget -= 1.5
                last.update({c: count for c in tiles})
            else:
                for c in tiles:
                    count += 1
                    plan[n].append(((c,), k, None, last.get(c, 0), count))
                    last[c] = count
                    budget -= 1
    return plan, last, used


SLOT, LONG_SLOT = 10, 14
PRODUCT_TAPS = range(2, TAPS, 2)
CONV_PLAN, TILE_DONE, PRODUCT_USED = conv_plan()

EARLY = (BG[0], BV[0]), (Z1[0], Z1[1])


def hybrid_trunk(nc, xT, w, vec, const, out):
    with ExitStack() as ctx:
        def sb(name, shape, dt=F32):
            return ctx.enter_context(nc.sbuf_tensor(name, shape, dt))

        def sem(name):
            return ctx.enter_context(nc.semaphore(name))

        raw = sb("raw", [P, RAW, UNIT])
        w_hi = sb("w_hi", [P, CUT, UNIT], F32R)
        w_lo = sb("w_lo", [P, CUT, UNIT], F32R)
        X = sb("X", [P, KD, S])
        H = sb("H", [P, KD, S])
        h_hi = sb("h_hi", [P, KD, S], F32R)
        h_lo = sb("h_lo", [P, KD, S], F32R)
        ya_hi = sb("ya_hi", [P, KD, S], F32R)
        ya_lo = sb("ya_lo", [P, KD, S], F32R)
        yb_hi = sb("yb_hi", [P, KD, S], F32R)
        yb_lo = sb("yb_lo", [P, KD, S], F32R)
        taps_hi = sb("taps_hi", [P, TAPS], F32R)
        taps_lo = sb("taps_lo", [P, TAPS], F32R)
        u_hi = sb("u_hi", [P, PAD + S], F32R)
        u_lo = sb("u_lo", [P, PAD + S], F32R)
        root = sb("root", [P, S])
        rinv = sb("rinv", [P, S])
        V_ = sb("params", [P, NV])
        C_ = sb("consts", [P, NC])
        ones = sb("ones", [P, P])
        eps = sb("eps", [P, 1])
        primed = sb("primed", [P, 8])
        mhalf = sb("mhalf", [P, 8])
        qscale = sb("qscale", [P, KD])
        ident = C_[:, IDN:IDN + P]
        dist = C_[:, DIST:DIST + 384]

        scratch = sb("scratch", [P, 12800])
        at = 0

        def part(n):
            nonlocal at
            v = scratch[:, at:at + n]
            at += n
            return v

        U = part(KD * (PAD + S)).rearrange("p (c t) -> p c t", c=KD)
        V = part(KD * S).rearrange("p (c t) -> p c t", c=KD)
        SZ = part(2 * KD * S).rearrange("p (c t) -> p c t", c=2 * KD)
        YP = part(KD * S).rearrange("p (c t) -> p c t", c=KD)
        SG = part(2 * S)
        AP = part(2 * (APAD + S)).rearrange("p (c t) -> p c t", c=2)
        W1 = part(2 * (APAD + S)).rearrange("p (c t) -> p c t", c=2)
        W2 = part(2 * (APAD + S)).rearrange("p (c t) -> p c t", c=2)
        FX = part(2 * 15).rearrange("p (c t) -> p c t", c=2)
        assert at <= 12800
        PR = SZ[:, 0:KD, :]
        SQ = YP
        at = 0
        SZ1 = part(KD * S).rearrange("p (c t) -> p c t", c=KD)
        qT = part(4 * S).rearrange("p (b c t) -> p b c t", b=2, c=2)
        kT = part(4 * S).rearrange("p (b c t) -> p b c t", b=2, c=2)
        vv = part(4 * S).rearrange("p (b t c) -> p b t c", b=2, t=2)
        qn = part(4 * S).rearrange("p (b t c) -> p b t c", b=2, t=2)
        sq1 = part(2 * S)
        neg = part(2 * 384).rearrange("p (b c) -> p b c", b=2)
        prob = part(2 * 384).rearrange("p (b c) -> p b c", b=2)
        pT = part(2 * 384).rearrange("p (b c) -> p b c", b=2)
        oz = part(2 * S).rearrange("p (b c) -> p b c", b=2)
        ss = part(2 * 8).rearrange("p (b c) -> p b c", b=2)
        sr = part(2 * 8).rearrange("p (b c) -> p b c", b=2)
        si = part(2 * 8).rearrange("p (b c) -> p b c", b=2)
        nmax = part(2 * 2).rearrange("p (b c) -> p b c", b=2)
        den = part(2 * 2).rearrange("p (b c) -> p b c", b=2)
        rden = part(2 * 2).rearrange("p (b c) -> p b c", b=2)
        assert at <= 12800

        bank = [ctx.enter_context(nc.psum_tensor(f"bank{i}", [P, 512], F32)) for i in range(8)]
        TR, SC, PV = bank[4], (bank[5], bank[6]), bank[7]

        x_in = [sem(f"x_in{i}") for i in range(2)]
        vec_in, const_in, stored = sem("vec_in"), sem("const_in"), sem("stored")
        raw_in = [sem(f"raw_in{i}") for i in range(RAW)]
        ones_set, pads_set, qs_set = sem("ones_set"), sem("pads_set"), sem("qs_set")
        hi_cut, lo_cut = sem("hi_cut"), sem("lo_cut")
        unit_done = sem("unit_done")
        sq_ready, folded = sem("sq_ready"), sem("folded")
        rms_sum = sem("rms_sum")
        root_ready, rinv_ready = sem("root_ready"), sem("rinv_ready")
        h_ready, hhi_ready, hlo_ready = sem("h_ready"), sem("hhi_ready"), sem("hlo_ready")
        late = sem("late")
        taps_cut, uhi_ready, ulo_ready = sem("taps_cut"), sem("uhi_ready"), sem("ulo_ready")
        diag_ready, conv_done, conv_out = sem("diag_ready"), sem("conv_done"), sem("conv_out")
        sig_ready, u_ready = sem("sig_ready"), sem("u_ready")
        a_ready, win, pooled, phi_ready, plo_ready = (
            sem("a_ready"), sem("win"), sem("pooled"), sem("phi_ready"), sem("plo_ready"))
        sz_ready, yp_ready = sem("sz_ready"), sem("yp_ready")
        ya_ready, yahi_ready, yalo_ready = sem("ya_ready"), sem("yahi_ready"), sem("yalo_ready")
        first_tap, product_ready, tap = sem("first_tap"), sem("product_ready"), sem("tap")
        mean_sum, centred, normed, swished = sem("mean_sum"), sem("centred"), sem("normed"), sem("swished")
        yb_ready, ybhi_ready, yblo_ready = sem("yb_ready"), sem("ybhi_ready"), sem("yblo_ready")
        bank_closed, x_updated = sem("bank_closed"), sem("x_updated")
        sz1_ready = sem("sz1_ready")
        qk_sq, qk_ss, qk_sr, qk_si, qk_normed = (
            sem("qk_sq"), sem("qk_ss"), sem("qk_sr"), sem("qk_si"), sem("qk_normed"))
        qk_turned, qk_out, v_out = sem("qk_turned"), sem("qk_out"), sem("v_out")
        scored, neg_ready, exped, rden_ready, prob_ready = (
            sem("scored"), sem("neg_ready"), sem("exped"), sem("rden_ready"), sem("prob_ready"))
        p_turned, p_out, pv_done, oz_ready, ozhi_ready, ozlo_ready = (
            sem("p_turned"), sem("p_out"), sem("pv_done"), sem("oz_ready"), sem("ozhi_ready"), sem("ozlo_ready"))

        block = ctx.enter_context(nc.Block())

        def diagonals(k):
            pair = (ya_hi, ya_lo) if k < CONV_CUT else (yb_hi, yb_lo)
            c, a = (k % CONV_CUT) // 2, P * (k % 2)
            return [t[:, c, a:a + P] for t in pair]

        def column(c, n=1):
            return V_[:, c:c + n]

        def halves(t, slot, half):
            return t[:, slot, half * (UNIT // 2):(half + 1) * (UNIT // 2)]

        @block.sync
        def _(sp):
            for i in range(2):
                sp.dma_start(X[:, 4 * i:4 * i + 4, :], xT[:, 4 * i:4 * i + 4, :]).then_inc(x_in[i], 16)
            for n in range(NU):
                m = n - RAW
                if m >= 0:
                    if m in NATIVE:
                        sp.wait_ge(unit_done, m + 1)
                    else:
                        sp.wait_ge(lo_cut, 2 * cut_index(m) + 2)
                sp.dma_start(raw[:, n % RAW, :], w[n, :, :]).then_inc(raw_in[n % RAW], 16)
                if n == 3:
                    sp.dma_start(C_[:, :], const).then_inc(const_in, 16)
            for m in range(4):
                sp.wait_ge(x_updated, 4 + m + 1)
                sp.dma_start(out[:, 2 * m:2 * m + 2, :], X[:, 2 * m:2 * m + 2, :]).then_inc(stored, 16)
            sp.wait_ge(stored, 64)

        @block.gpsimd
        def _(pool):
            nc.gpsimd.memset(ones[:, :], 1.0 / D).then_inc(ones_set, 1)
            nc.gpsimd.memset(eps[:, :], EPS).then_inc(ones_set, 1)
            nc.gpsimd.memset(mhalf[:, :], -0.5).then_inc(pads_set, 1)
            nc.gpsimd.memset(U[:, :, 0:PAD], 0.0).then_inc(pads_set, 1)
            nc.gpsimd.memset(AP[:, :, 0:APAD], 0.0).then_inc(pads_set, 1)
            pool.wait_ge(vec_in, 16)
            pool.wait_ge(const_in, 16)
            nc.gpsimd.tensor_tensor(qscale[:, :], C_[:, QSC:QSC + KD], column(GQ).to_broadcast([P, KD]),
                                    ALU.mult).then_inc(qs_set, 1)
            pool.wait_ge(pads_set, 3)
            for r in range(8):
                pool.wait_ge(qk_ss, r + 1)
                nc.gpsimd.tensor_scalar(sr[:, r % 2, :], ss[:, r % 2, :], EPS, None, ALU.add).then_inc(qk_sr, 1)
                pool.wait_ge(qk_sr, r + 1)
                nc.gpsimd.tensor_tensor(si[:, r % 2, :], sr[:, r % 2, :], mhalf[:, :], ALU.pow).then_inc(qk_si, 1)

        @block.scalar
        def _(act):
            def cut_hi(n):
                if n >= NU or n in NATIVE:
                    return
                s = cut_index(n)
                act.wait_ge(raw_in[n % RAW], 16 * (n // RAW + 1))
                if s >= CUT:
                    act.wait_ge(unit_done, CUTS[s - CUT] + 1)
                for half in range(2):
                    nc.scalar.copy(halves(w_hi, s % CUT, half), halves(raw, n % RAW, half)).then_inc(hi_cut, 1)

            def square(group, m, source):
                nc.scalar.activation(SQ[:, 2 * m:2 * m + 2, :], source[:, 2 * m:2 * m + 2, :], ACT.Square).then_inc(sq_ready, 1)

            def take_root(source, n):
                act.wait_ge(rms_sum, n)
                nc.scalar.activation(root[:, :], source[:, 0:S], ACT.Sqrt, bias=eps[:, 0:1]).then_inc(root_ready, 1)

            primings = 0

            def prime(func):
                nonlocal primings
                nc.scalar.activation(primed[:, primings:primings + 1], eps[:, :], func)
                primings += 1

            def high_h(step, m):
                act.wait_ge(h_ready, 4 * step + m + 1)
                to = h_hi if step % 2 else ya_hi
                nc.scalar.copy(to[:, 2 * m:2 * m + 2, :], H[:, 2 * m:2 * m + 2, :]).then_inc(hhi_ready, 1)

            def late_gate(layer, i, dst, func, done):
                act.wait_ge(late, 2 * layer + i + 1)
                nc.scalar.activation(dst, dst, func).then_inc(done, 1)

            act.dma_start(V_[:, :], vec).then_inc(vec_in, 16)
            act.wait_ge(ones_set, 2)
            prime(ACT.Sqrt)
            for m in range(4):
                if m % 2 == 0:
                    act.wait_ge(x_in[m // 2], 16)
                square(0, m, X)
            for m in range(4):
                high_h(0, m)
            cut_hi(1)
            nc.scalar.copy(taps_hi[:, :], column(CW + TAPS * CONV_PE, TAPS)).then_inc(taps_cut, 1)
            take_root(bank[4], 1)
            prime(ACT.Sigmoid)
            cut_hi(2)
            for m in range(4):
                high_h(1, m)
            cut_hi(CUTS[2])
            late_gate(0, 0, SG[:, :], ACT.Sigmoid, sig_ready)

            def build_diagonals(first, last):
                for k in range(first, min(last, TAPS)):
                    for part, t in zip(diagonals(k), (taps_hi, taps_lo)):
                        nc.scalar.mul(part, ident, t[:, k:k + 1].bitcast(F32)).then_inc(diag_ready, 1)

            for n in range(1, OA[0] + 1):
                if n + 2 != CUTS[2]:
                    cut_hi(n + 2)
                if n in BUILD:
                    if n == BUILD[0]:
                        act.wait_ge(taps_cut, 2)
                        act.wait_ge(const_in, 16)
                        act.wait_ge(unit_done, BV[0] + 1)
                    build_diagonals((n - BUILD[0]) * PER_BUILD, (n - BUILD[0] + 1) * PER_BUILD)
                if n == ZA[0]:
                    act.wait_ge(tap, PRODUCT_USED[-1])
                if n - 1 in ZA:
                    i = n - 1 - ZA[0]
                    if OA[i] not in NATIVE:
                        act.wait_ge(ya_ready, i + 1)
                        nc.scalar.copy(ya_hi[:, 2 * i:2 * i + 2, :], SZ[:, 2 * i:2 * i + 2, :]).then_inc(yahi_ready, 1)
                if n in ZB:
                    g = n - ZB[0]
                    act.wait_ge(pooled, g + 1)
                    if g == 0:
                        act.wait_ge(conv_done, 2)
                    nc.scalar.copy(yb_hi[:, 2 * g:2 * g + 2, :], YP[:, 2 * g:2 * g + 2, :]).then_inc(phi_ready, 1)
                for tiles, k, product, _, _ in CONV_PLAN.get(n, ()):
                    if product is None:
                        continue
                    if product >= PRODUCTS:
                        act.wait_ge(tap, PRODUCT_USED[product - PRODUCTS])
                    for i, c in enumerate(tiles):
                        last = nc.scalar.mul(PR[:, 2 * (product % PRODUCTS) + i, :], U[:, c, k:k + S],
                                             column(CW + TAPS * c + k))
                    last.then_inc(product_ready, 1)
                if n in BG:
                    i = n // 2
                    act.wait_ge(unit_done, n + 1)
                    if i >= 1:
                        act.wait_ge(u_ready, i)
                    nc.scalar.activation(SG[:, :], bank[n % 4][:, :], ACT.Sigmoid).then_inc(sig_ready, 1)
                if n in BG[1:] or n == A[0]:
                    for c in (n - 2, n - 1):
                        if c == n - 2:
                            act.wait_ge(u_ready, n // 2)
                        if c == CONV_PE:
                            nc.scalar.copy(u_hi[:, :], U[:, c, :]).then_inc(uhi_ready, 1)
                        else:
                            nc.scalar.activation(V[:, c, :], U[:, c, 0:S], ACT.Identity, bias=column(CB + c),
                                                 scale=column(CW + TAPS * c)).then_inc(first_tap, 1)
                if n in A:
                    g = n - A[0]
                    act.wait_ge(unit_done, n + 1)
                    if g == 0:
                        act.wait_ge(pads_set, 3)
                    else:
                        act.wait_ge(pooled, g)
                    nc.scalar.copy(AP[:, :, APAD:APAD + S],
                                   bank[n % 4][:, :].rearrange("p (c t) -> p c t", c=2)).then_inc(a_ready, 1)
                if n in ZB or n in ZA:
                    i = n - ZB[0] if n in ZB else n - ZA[0]
                    c = (KD if n in ZB else 0) + 2 * i
                    act.wait_ge(unit_done, n + 1)
                    nc.scalar.activation(SZ[:, c:c + 2, :], bank[n % 4][:, :].rearrange("p (c t) -> p c t", c=2),
                                         ACT.Silu).then_inc(sz_ready, 1)
                if n == ZB[1]:
                    act.wait_ge(conv_done, 2)
                    nc.scalar.activation(V[:, CONV_PE, :], bank[5][:, 0:S], ACT.Identity,
                                         bias=column(CB + CONV_PE)).then_inc(conv_out, 1)
                if n == PW:
                    act.wait_ge(unit_done, n + 1)
                    act.wait_ge(plo_ready, 4)
                    for e in range(KD):
                        nc.scalar.mul(YP[:, e, :], bank[4 + e // 2][:, S * (e % 2):S * (e % 2) + S],
                                      column(PS + e)).then_inc(yp_ready, 1)

            act.wait_ge(ya_ready, 4)
            for m in range(4):
                act.wait_ge(centred, m + 1)
                square(1, m, V)
            cut_hi(OA[0] + 3)
            prime(ACT.Sqrt)
            cut_hi(OB[0])
            take_root(bank[2], 2)
            prime(ACT.Silu)
            for m in range(5):
                for c in (2 * m, 2 * m + 1) if m < 4 else ():
                    act.wait_ge(normed, m + 1)
                    nc.scalar.activation(V[:, c, :], V[:, c, :], ACT.Silu, bias=column(CBETA + c),
                                         scale=column(CG + c)).then_inc(swished, 1)
                if m >= 1 and OB[m - 1] not in NATIVE:
                    act.wait_ge(yb_ready, m)
                    nc.scalar.copy(yb_hi[:, 2 * m - 2:2 * m, :], SZ[:, KD + 2 * m - 2:KD + 2 * m, :]).then_inc(ybhi_ready, 1)
            for n in range(OB[1], Z1[1]):
                cut_hi(n)

            prime(ACT.Sqrt)
            for m in range(4):
                act.wait_ge(x_updated, m + 1)
                square(2, m, X)
                high_h(2, m)
            cut_hi(Z1[1])
            take_root(bank[0], 3)
            cut_hi(Z1[2])
            for m in range(4):
                high_h(3, m)
            cut_hi(Z1[3])

            def head_exp(h):
                for t, (a, b) in enumerate(((0, 128), (128, 384))):
                    act.wait_ge(neg_ready, 2 * h + t + 1)
                    if h >= 2 and t == 0:
                        act.wait_ge(p_turned, h - 1)
                    nc.scalar.activation(prob[:, h % 2, a:b], neg[:, h % 2, a:b], ACT.Exp, scale=-1.0,
                                         bias=nmax[:, h % 2, t:t + 1],
                                         accum_out=den[:, h % 2, t:t + 1]).then_inc(exped, 1)

            def head_turn_out(h):
                act.wait_ge(p_turned, h + 1)
                if h >= 2:
                    act.wait_ge(pv_done, h - 1)
                nc.scalar.copy(pT[:, h % 2, :], TR[:, 0:384]).then_inc(p_out, 1)

            def heads_hi(pair):
                act.wait_ge(oz_ready, pair + 1)
                nc.scalar.copy(ya_hi[:, pair, :], oz[:, pair % 2, :]).then_inc(ozhi_ready, 1)

            def attention_step(j, s):
                for quad, at in ((j - 1, s + STEPS), (j, s)):
                    if not 0 <= quad < 4:
                        continue
                    scores, turns, values = head_steps(quad)
                    for i in range(4):
                        if at == scores[i] + 1:
                            head_exp(4 * quad + i)
                        if at == turns[i]:
                            head_turn_out(4 * quad + i)
                    for i in (1, 3):
                        if at == values[i] + 2:
                            heads_hi(2 * quad + i // 2)

            for i, n in enumerate(Z1):
                if i > 1:
                    cut_hi(n + 2)
                to = SZ1[:, 2 * i:2 * i + 2, :]
                if n in EARLY[1]:
                    late_gate(1, i, to, ACT.Silu, sz1_ready)
                else:
                    act.wait_ge(unit_done, n + 1)
                    nc.scalar.activation(to, bank[n % 4][:, :].rearrange("p (c t) -> p c t", c=2),
                                         ACT.Silu).then_inc(sz1_ready, 1)

            def qk_squares(n, j, isq):
                r = 2 * j + isq
                act.wait_ge(unit_done, n + 1)
                if r >= 1:
                    act.wait_ge(qk_ss, r)
                nc.scalar.activation(sq1[:, :], bank[n % 4][:, :], ACT.Square, scale=DH ** -0.5).then_inc(qk_sq, 1)

            def qk_turn_out(j, isq):
                r = 2 * j + isq
                act.wait_ge(qk_turned, r + 1)
                if isq:
                    act.wait_ge(qs_set, 1)
                for c in range(2):
                    nc.scalar.mul((qT if isq else kT)[:, j % 2, c, :], TR[:, c * S:c * S + S],
                                  qscale[:, 2 * j + c:2 * j + c + 1] if isq else column(GK)).then_inc(qk_out, 1)

            for j in range(4):
                for u, n in enumerate((KU[j], QU[j], VU[j])):
                    for step in range(8):
                        s = 8 * u + step
                        if j and s == QT_AT - STEPS:
                            qk_turn_out(j - 1, 1)
                        attention_step(j - 1, s)
                        if step == CUT_HI_AT:
                            cut_hi(n + 2)
                        if s == KT_AT:
                            qk_turn_out(j, 0)
                    if u < 2:
                        qk_squares(n, j, u)
                    else:
                        act.wait_ge(unit_done, n + 1)
                        if j >= 2:
                            act.wait_ge(pv_done, 4 * (j - 1))
                        nc.scalar.copy(vv[:, j % 2, :, :], bank[n % 4][:, :].rearrange("p (t c) -> p t c", t=2)
                                       ).then_inc(v_out, 1)
            for s in range(STEPS + 12):
                if s == QT_AT - STEPS:
                    qk_turn_out(3, 1)
                attention_step(3 + s // STEPS, s % STEPS)
                if s == 2:
                    cut_hi(O1[0] + 2)
                if s == 10:
                    cut_hi(O1[0] + 3)

        @block.vector
        def _(dve):
            def cut_lo(n, parts=(0, 1)):
                if n >= NU or n in NATIVE:
                    return
                s = cut_index(n)
                for half in parts:
                    dve.wait_ge(hi_cut, 2 * s + half + 1)
                    nc.vector.tensor_tensor(halves(w_lo, s % CUT, half), halves(raw, n % RAW, half),
                                            halves(w_hi, s % CUT, half).bitcast(F32), ALU.subtract).then_inc(lo_cut, 1)

            def gained(layer, m):
                for c in (2 * m, 2 * m + 1):
                    last = nc.vector.tensor_scalar(H[:, c, :], X[:, c, :], column((G0, G1)[layer] + c), None, ALU.mult)
                last.then_inc(h_ready, 1)

            def low_h(step, m):
                dve.wait_ge(hhi_ready, 4 * step + m + 1)
                hi, lo = (h_hi, h_lo) if step % 2 else (ya_hi, ya_lo)
                nc.vector.tensor_tensor(lo[:, 2 * m:2 * m + 2, :], H[:, 2 * m:2 * m + 2, :],
                                        hi[:, 2 * m:2 * m + 2, :].bitcast(F32), ALU.subtract).then_inc(hlo_ready, 1)

            folds = 0

            def fold(group, pairs):
                nonlocal folds
                steps = ((0, 4, 4), (0, 2, 2), (0, 1, 1)) if pairs == 4 else ((0, 2, 2), (0, 4, 2))
                for i, (a, b, n) in enumerate(steps):
                    if pairs == 4 and i == 0:
                        dve.wait_ge(sq_ready, 4 * group + 4)
                    elif pairs == 3:
                        dve.wait_ge(sq_ready, 4 * group + i + 2)
                    if i:
                        dve.wait_ge(folded, folds)
                    nc.vector.tensor_tensor(SQ[:, a:a + n, :], SQ[:, a:a + n, :], SQ[:, b:b + n, :],
                                            ALU.add).then_inc(folded, 1)
                    folds += 1

            def take_inverse(n):
                dve.wait_ge(root_ready, n)
                nc.vector.reciprocal(rinv[:, :], root[:, :]).then_inc(rinv_ready, 1)
                dve.wait_ge(rinv_ready, n)

            def over_rms(layer):
                if layer == 0:
                    dve.wait_ge(unit_done, BG[0] + 1)
                for m in range(5):
                    if m < 4:
                        nc.vector.tensor_tensor(H[:, 2 * m:2 * m + 2, :], H[:, 2 * m:2 * m + 2, :],
                                                rinv[:, :].unsqueeze(1).to_broadcast([P, 2, S]),
                                                ALU.mult).then_inc(h_ready, 1)
                    if m:
                        low_h(2 * layer + 1, m - 1)

            def scale_late(layer, i, dst):
                n = EARLY[layer][i]
                dve.wait_ge(unit_done, n + 1)
                nc.vector.tensor_tensor(dst, bank[n % 4][:, :].rearrange("p (c t) -> p c t", c=2),
                                        rinv[:, :].unsqueeze(1).to_broadcast([P, 2, S]), ALU.mult).then_inc(late, 1)

            SG2 = SG[:, :].rearrange("p (c t) -> p c t", c=2)
            dve.wait_ge(vec_in, 16)
            for m in range(4):
                if m % 2 == 0:
                    dve.wait_ge(x_in[m // 2], 16)
                gained(0, m)
            fold(0, 4)
            for m in range(4):
                low_h(0, m)
            cut_lo(1)
            dve.wait_ge(taps_cut, 1)
            nc.vector.tensor_tensor(taps_lo[:, :], column(CW + TAPS * CONV_PE, TAPS), taps_hi[:, :].bitcast(F32),
                                    ALU.subtract).then_inc(taps_cut, 1)
            take_inverse(1)
            cut_lo(2)
            over_rms(0)
            scale_late(0, 0, SG2)

            def window_sums(g):
                width = WINDOWS[g]
                dve.wait_ge(a_ready, g + 1)
                src = AP
                count = sum(lv + 2 for lv in range(g))
                for lv in range(g + 1):
                    shift = 1 << lv
                    lo = APAD if lv == g else 2 * shift
                    dst = (W1, W2)[lv % 2]
                    if lv:
                        dve.wait_ge(win, count + lv)
                    nc.vector.tensor_tensor(dst[:, :, lo:APAD + S], src[:, :, lo:APAD + S],
                                            src[:, :, lo - shift:APAD + S - shift], ALU.add).then_inc(win, 1)
                    src = dst
                dve.wait_ge(win, count + g + 1)
                F = width - 1
                inv = C_[:, IC + 15 * g:IC + 15 * g + F].unsqueeze(1).to_broadcast([P, 2, F])
                nc.vector.scalar_tensor_tensor(YP[:, 2 * g:2 * g + 2, F:S], src[:, :, APAD + F:APAD + S], 1.0 / width,
                                               AP[:, :, APAD + F:APAD + S], ALU.mult, ALU.subtract)
                if g == 0:
                    dve.wait_ge(const_in, 16)
                nc.vector.tensor_tensor(FX[:, :, 0:F], src[:, :, APAD:APAD + F], inv, ALU.mult).then_inc(win, 1)
                dve.wait_ge(win, count + g + 2)
                nc.vector.tensor_tensor(YP[:, 2 * g:2 * g + 2, 0:F], FX[:, :, 0:F], AP[:, :, APAD:APAD + F],
                                        ALU.subtract).then_inc(pooled, 1)

            def taps(n):
                for tiles, k, product, ready, _ in CONV_PLAN.get(n, ()):
                    c = tiles[0]
                    if ready:
                        dve.wait_ge(tap, ready)
                    else:
                        dve.wait_ge(first_tap, tiles[-1] + 1)
                    if product is None:
                        nc.vector.scalar_tensor_tensor(V[:, c, :], U[:, c, k:k + S], column(CW + TAPS * c + k),
                                                       V[:, c, :], ALU.mult, ALU.add).then_inc(tap, 1)
                    else:
                        dve.wait_ge(product_ready, product + 1)
                        b = 2 * (product % PRODUCTS)
                        nc.vector.tensor_tensor(V[:, c:c + 2, :], V[:, c:c + 2, :], PR[:, b:b + 2, :],
                                                ALU.add).then_inc(tap, 1)

            assert BG[0] in NATIVE
            dve.wait_ge(pads_set, 3)
            def centre():
                dve.wait_ge(mean_sum, 1)
                for m in range(4):
                    nc.vector.tensor_tensor(V[:, 2 * m:2 * m + 2, :], V[:, 2 * m:2 * m + 2, :],
                                            bank[1][:, 0:S].unsqueeze(1).to_broadcast([P, 2, S]),
                                            ALU.subtract).then_inc(centred, 1)

            for n in range(1, OA[0] + 1):
                if n < OA[0]:
                    cut_lo(n + 2)
                m = n - 1
                if m in BV:
                    i = m // 2
                    dve.wait_ge(sig_ready, i + 1)
                    dve.wait_ge(unit_done, m + 1)
                    value = bank[m % 4][:, :].rearrange("p (c t) -> p c t", c=2)
                    if m in EARLY[0]:
                        scale_late(0, 1, W1[:, :, 0:S])
                        dve.wait_ge(late, 2)
                        value = W1[:, :, 0:S]
                    nc.vector.tensor_tensor(U[:, 2 * i:2 * i + 2, PAD:PAD + S], value, SG2, ALU.mult).then_inc(u_ready, 1)
                if n == A[1]:
                    dve.wait_ge(uhi_ready, 1)
                    nc.vector.tensor_tensor(u_lo[:, :], U[:, CONV_PE, :], u_hi[:, :].bitcast(F32),
                                            ALU.subtract).then_inc(ulo_ready, 1)
                if m in A:
                    window_sums(m - A[0])
                if n in ZB:
                    g = n - ZB[0]
                    dve.wait_ge(phi_ready, g + 1)
                    nc.vector.tensor_tensor(yb_lo[:, 2 * g:2 * g + 2, :], YP[:, 2 * g:2 * g + 2, :],
                                            yb_hi[:, 2 * g:2 * g + 2, :].bitcast(F32), ALU.subtract).then_inc(plo_ready, 1)
                if m in ZA:
                    i = m - ZA[0]
                    dve.wait_ge(sz_ready, 4 + i + 1)
                    dve.wait_ge(yp_ready, 2 * i + 2)
                    nc.vector.tensor_tensor(SZ[:, 2 * i:2 * i + 2, :], SZ[:, 2 * i:2 * i + 2, :],
                                            YP[:, 2 * i:2 * i + 2, :], ALU.mult).then_inc(ya_ready, 1)
                taps(n)
                if n == OA[0]:
                    centre()
                    cut_lo(n + 2)
                if m in ZA and OA[i] not in NATIVE:
                    dve.wait_ge(yahi_ready, pairs_cut(OA, i + 1))
                    nc.vector.tensor_tensor(ya_lo[:, 2 * i:2 * i + 2, :], SZ[:, 2 * i:2 * i + 2, :],
                                            ya_hi[:, 2 * i:2 * i + 2, :].bitcast(F32), ALU.subtract).then_inc(yalo_ready, 1)

            fold(1, 4)
            cut_lo(OA[0] + 3)
            take_inverse(2)
            dve.wait_ge(sq_ready, 8)

            def normalise(m):
                nc.vector.tensor_tensor(V[:, 2 * m:2 * m + 2, :], V[:, 2 * m:2 * m + 2, :],
                                        rinv[:, :].unsqueeze(1).to_broadcast([P, 2, S]), ALU.mult).then_inc(normed, 1)

            def gate_yb(m):
                dve.wait_ge(swished, 2 * m + 2)
                nc.vector.tensor_tensor(SZ[:, KD + 2 * m:KD + 2 * m + 2, :], SZ[:, KD + 2 * m:KD + 2 * m + 2, :],
                                        V[:, 2 * m:2 * m + 2, :], ALU.mult).then_inc(yb_ready, 1)

            def low_yb(m):
                if OB[m] in NATIVE:
                    return
                dve.wait_ge(ybhi_ready, pairs_cut(OB, m + 1))
                nc.vector.tensor_tensor(yb_lo[:, 2 * m:2 * m + 2, :], SZ[:, KD + 2 * m:KD + 2 * m + 2, :],
                                        yb_hi[:, 2 * m:2 * m + 2, :].bitcast(F32), ALU.subtract).then_inc(yblo_ready, 1)

            dve.wait_ge(sz_ready, 8)
            normalise(0)
            normalise(1)
            cut_lo(OB[0], (0,))
            gate_yb(0)
            normalise(2)
            low_yb(0)
            cut_lo(OB[0], (1,))
            gate_yb(1)
            normalise(3)
            low_yb(1)
            for m in (2, 3):
                gate_yb(m)
                low_yb(m)
            for n in range(OB[1], Z1[1]):
                cut_lo(n)

            def residual(m, layer):
                if m < 3:
                    dve.wait_ge(bank_closed, 3 * layer + m + 1)
                else:
                    dve.wait_ge(unit_done, (Z1[0], NU)[layer])
                nc.vector.tensor_tensor(X[:, 2 * m:2 * m + 2, :], X[:, 2 * m:2 * m + 2, :],
                                        bank[(4, 0)[layer] + m][:, :].rearrange("p (c t) -> p c t", c=2),
                                        ALU.add).then_inc(x_updated, 1)

            for m in range(5):
                if m < 4:
                    residual(m, 0)
                    dve.wait_ge(x_updated, m + 1)
                    gained(1, m)
                if m:
                    low_h(2, m - 1)
                if m == 2:
                    fold(2, 3)
            cut_lo(Z1[1])
            take_inverse(3)
            cut_lo(Z1[2])
            over_rms(1)
            cut_lo(Z1[3])

            def head_bias(h):
                slope = 2.0 ** (-8.0 * (h + 1) / HEADS)
                dve.wait_ge(scored, h + 1)
                if h >= 2:
                    dve.wait_ge(exped, 2 * h - 2)
                for t, (a, b) in enumerate(((0, 128), (128, 384))):
                    nc.vector.tensor_tensor_reduce(neg[:, h % 2, a:b], dist[:, a:b], SC[h % 2][:, a:b], slope, 3.0e38,
                                                   ALU.add, ALU.min,
                                                   nmax[:, h % 2, t:t + 1]).then_inc(neg_ready, 1)

            def head_scale(h):
                dve.wait_ge(exped, 2 * h + 2)
                nc.vector.reciprocal(rden[:, h % 2, :], den[:, h % 2, :]).then_inc(rden_ready, 1)
                dve.wait_ge(rden_ready, h + 1)
                for t, (a, b) in enumerate(((0, 128), (128, 384))):
                    nc.vector.tensor_scalar(prob[:, h % 2, a:b], prob[:, h % 2, a:b], rden[:, h % 2, t:t + 1], None,
                                            ALU.mult).then_inc(prob_ready, 1)

            def heads_gate(pair):
                dve.wait_ge(pv_done, 2 * pair + 2)
                if pair >= 2:
                    dve.wait_ge(ozlo_ready, pair - 1)
                    dve.wait_ge(ozhi_ready, pair - 1)
                if pair == 0:
                    dve.wait_ge(sz1_ready, 4)
                nc.vector.tensor_tensor(oz[:, pair % 2, :], PV[:, 0:S], SZ1[:, pair, :], ALU.mult).then_inc(oz_ready, 1)

            def heads_lo(pair):
                dve.wait_ge(ozhi_ready, pair + 1)
                nc.vector.tensor_tensor(ya_lo[:, pair, :], oz[:, pair % 2, :], ya_hi[:, pair, :].bitcast(F32),
                                        ALU.subtract).then_inc(ozlo_ready, 1)

            def attention_step(j, s):
                for quad, at in ((j - 1, s + STEPS), (j, s)):
                    if not 0 <= quad < 4:
                        continue
                    scores, turns, values = head_steps(quad)
                    for i in range(4):
                        if at == scores[i]:
                            head_bias(4 * quad + i)
                        if at == scores[i] + 3:
                            head_scale(4 * quad + i)
                    for i in (1, 3):
                        if at == values[i] + 1:
                            heads_gate(2 * quad + i // 2)
                        if at == values[i] + 3:
                            heads_lo(2 * quad + i // 2)

            for i, n in enumerate(Z1):
                if i > 1:
                    cut_lo(n + 2)
                if n in EARLY[1]:
                    scale_late(1, i, SZ1[:, 2 * i:2 * i + 2, :])

            def qk_sums(j, isq):
                r = 2 * j + isq
                dve.wait_ge(qk_sq, r + 1)
                nc.vector.tensor_reduce(ss[:, isq, :], sq1[:, :].rearrange("p (h d) -> p h d", d=DH),
                                        AX_X, ALU.add).then_inc(qk_ss, 1)

            def qk_norm(n, j, isq):
                r = 2 * j + isq
                src = bank[n % 4][:, :].rearrange("p (h d) -> p h d", d=DH)
                dve.wait_ge(qk_si, r + 1)
                if r >= 2:
                    dve.wait_ge(qk_turned, r - 1)
                nc.vector.tensor_tensor(qn[:, isq, :, :].rearrange("p t (h d) -> p (t h) d", d=DH), src,
                                        si[:, isq, :].unsqueeze(2).to_broadcast([P, 8, DH]),
                                        ALU.mult).then_inc(qk_normed, 1)

            for j in range(4):
                for u, n in enumerate((KU[j], QU[j], VU[j])):
                    for step in range(8):
                        attention_step(j - 1, 8 * u + step)
                        if step == SUM_AT and u > 0:
                            qk_sums(j, u - 1)
                        if step == NORM_AT and u > 0:
                            qk_norm(n - 1, j, u - 1)
                        if step == CUT_LO_AT:
                            cut_lo(n + 2)
            for s in range(STEPS + 12):
                attention_step(3 + s // STEPS, s % STEPS)
                if s == 2:
                    cut_lo(O1[0] + 2)
                if s == 10:
                    cut_lo(O1[0] + 3)
            for m in range(4):
                residual(m, 1)

        @block.tensor
        def _(pe):
            def product(dst, stationary, moving, start, stop):
                (wh, wl), (ah, al) = stationary, moving
                nc.tensor.matmul(dst, wh, ah, start=start, stop=False, skip_group_check=True)
                nc.tensor.matmul(dst, wh, al, start=False, stop=False, skip_group_check=True)
                return nc.tensor.matmul(dst, wl, ah, start=False, stop=stop, skip_group_check=True)

            def arrived(n, half):
                if n in NATIVE:
                    if half == 0:
                        pe.wait_ge(raw_in[n % RAW], 16 * (n // RAW + 1))
                else:
                    pe.wait_ge(lo_cut, 2 * cut_index(n) + half + 1)

            def piece(n, a, b):
                s = cut_index(n) % CUT
                return raw[:, n % RAW, a:b], (w_hi[:, s, a:b], w_lo[:, s, a:b])

            def channel_step(n, k, h_wait=None):
                if k % 4 == 0:
                    arrived(n, k // 4)
                if h_wait == 0 and n in NATIVE:
                    if k % 2 == 0:
                        pe.wait_ge(h_ready, k // 2 + 1)
                elif h_wait is not None and k % 2 == 0:
                    pe.wait_ge(hlo_ready, 4 * h_wait + k // 2 + 1)
                hi, lo = (ya_hi, ya_lo) if n in EARLY[0] + EARLY[1] else (h_hi, h_lo)
                for c in range(2):
                    a = k * UC + c * P
                    wr, wp = piece(n, a, a + P)
                    dst = bank[n % 4][:, c * S:c * S + S]
                    start, stop = k == 0 and c == 0, k == KD - 1
                    if n in NATIVE:
                        last = nc.tensor.matmul(dst, wr, H[:, k, :], start=start, stop=stop, skip_group_check=True)
                    else:
                        last = product(dst, wp, (hi[:, k, :], lo[:, k, :]), start, stop)
                if k == KD - 1:
                    last.then_inc(unit_done, 1)

            def token_step(n, k):
                if k % 4 == 0:
                    arrived(n, k // 4)
                _, (wh, wl) = piece(n, k * UC, (k + 1) * UC)
                for t in range(TT):
                    ah, al = h_hi[:, k, t * P:t * P + P], h_lo[:, k, t * P:t * P + P]
                    last = product(bank[n % 4][:, t * UC:t * UC + UC], (ah, al), (wh, wl),
                                   k == 0 and t == 0, k == KD - 1)
                if k == KD - 1:
                    last.then_inc(unit_done, 1)

            def out_product(n, kt, m, y, tile, acc, start, stop):
                a = kt * D + m * P
                wr, wp = piece(n, a, a + P)
                y_hi, y_lo = y
                dst = bank[acc + m // 2][:, S * (m % 2):S * (m % 2) + S]
                if n in NATIVE:
                    return nc.tensor.matmul(dst, wr, SZ[:, (KD if n in OB else 0) + tile, :],
                                            start=start and m % 2 == 0, stop=stop, skip_group_check=True)
                return product(dst, wp,
                               (y_hi[:, tile, :], y_lo[:, tile, :]), start and m % 2 == 0, stop)

            pe.wait_ge(ones_set, 1)
            for _ in range(WARM):
                nc.tensor.matmul(bank[7][:, 0:P], ones[:, :], ones[:, :], start=True, stop=True, skip_group_check=True)

            def square_sums(folds, tiles, dst, last):
                if folds:
                    pe.wait_ge(folded, folds)
                else:
                    pe.wait_ge(sq_ready, 12)
                for c in tiles:
                    summed = nc.tensor.matmul(dst[:, 0:S], ones[:, :], SQ[:, c, :], start=(c == 0),
                                              stop=(last and c == tiles[-1]), skip_group_check=True)
                if last:
                    summed.then_inc(rms_sum, 1)

            def conv_taps(a, b):
                pe.wait_ge(ulo_ready, 1)
                pe.wait_ge(diag_ready, 2 * b)
                for k in range(a, b):
                    last = product(bank[5][:, 0:S], diagonals(k), (u_hi[:, k:k + S], u_lo[:, k:k + S]),
                                   k == 0, k == TAPS - 1)
                last.then_inc(conv_done, 1)

            for n in range(PW):
                if n >= 4:
                    m = n - 4
                    if m in BG and m not in EARLY[0]:
                        pe.wait_ge(sig_ready, m // 2 + 1)
                    elif m in BG:
                        pe.wait_ge(late, 1)
                    elif m in BV:
                        pe.wait_ge(u_ready, m // 2 + 1)
                    elif m in A:
                        pe.wait_ge(a_ready, m - A[0] + 1)
                for k in range(KD):
                    channel_step(n, k, {0: 0, 1: 0, 2: 1}.get(n))
                    if n == 0 and k == 3:
                        square_sums(3, (0,), bank[4], True)
                if n in (A[2], ZB[0]):
                    conv_taps(*((0, CONV_CUT) if n == A[2] else (CONV_CUT, TAPS)))

            n = PW
            for g in range(4):
                if g % 2 == 0:
                    arrived(n, g // 2)
                pe.wait_ge(plo_ready, g + 1)
                if g == 0:
                    pe.wait_ge(root_ready, 1)
                    pe.wait_ge(conv_out, 1)
                for ct in range(2):
                    for e in range(2):
                        a = (2 * g + ct) * UC + e * P
                        wr, wp = piece(n, a, a + P)
                        last = product(bank[4 + g][:, e * S:e * S + S], wp,
                                       (yb_hi[:, 2 * g + ct, :], yb_lo[:, 2 * g + ct, :]), ct == 0 and e == 0, ct == 1)
            last.then_inc(unit_done, 1)

            for n in ZA:
                if n != ZA[3]:
                    pe.wait_ge(sz_ready, n - ZA[0] + 2)
                for k in range(KD):
                    channel_step(n, k)

            def channel_mean(tiles):
                for c in tiles:
                    if c == CONV_PE:
                        pe.wait_ge(conv_out, 1)
                    else:
                        pe.wait_ge(tap, TILE_DONE[c])
                    last = nc.tensor.matmul(bank[1][:, 0:S], ones[:, :], V[:, c, :], start=(c == CONV_PE), stop=(c == 6),
                                            skip_group_check=True)
                if tiles[-1] == 6:
                    last.then_inc(mean_sum, 1)

            pe.wait_ge(yp_ready, KD)
            for i, n in enumerate(OA):
                if n in NATIVE:
                    pe.wait_ge(ya_ready, i + 1)
                else:
                    pe.wait_ge(yalo_ready, pairs_cut(OA, i + 1))
                for kt in range(2):
                    arrived(n, kt)
                    for m in range(KD):
                        last = out_product(n, kt, m, (ya_hi, ya_lo), 2 * i + kt, 4, i == 0 and kt == 0, False)
                    if i == 2 and kt == 0:
                        square_sums(6, (0,), bank[2], True)
                last.then_inc(unit_done, 1)
                if i == 0:
                    pe.wait_ge(sz_ready, 6)
                    channel_mean((CONV_PE, 0, 1, 2, 3, 4, 5, 6))

            for i in range(2):
                n = OB[i]
                if n in NATIVE:
                    pe.wait_ge(yb_ready, i + 1)
                else:
                    pe.wait_ge(yblo_ready, pairs_cut(OB, i + 1))
                for kt in range(2):
                    arrived(n, kt)
                    for m in range(KD):
                        last = out_product(n, kt, m, (yb_hi, yb_lo), 2 * i + kt, 4, False, False)
                last.then_inc(unit_done, 1)

            def closing(units, y, first_tile, acc, ready):
                pe.wait_ge(ready[0], ready[1])
                for n in units:
                    assert n not in NATIVE
                    arrived(n, 1)
                for m in range(KD):
                    for u, n in enumerate(units):
                        for kt in range(2):
                            last = out_product(n, kt, m, y, first_tile + 2 * u + kt, acc, False, u == len(units) - 1 and kt == 1)
                        if m == KD - 1 and u == 0 and len(units) == 2:
                            last.then_inc(unit_done, 1)
                    if m % 2 == 1 and m < KD - 1:
                        last.then_inc(bank_closed, 1)
                last.then_inc(unit_done, 1)

            closing(OB[2:], (yb_hi, yb_lo), 4, 4, (yblo_ready, pairs_cut(OB, 4)))

            for n in Z1:
                if n % 4 == 0:
                    pe.wait_ge(root_ready, 3)
                for k in range(KD):
                    channel_step(n, k, {Z1[0]: 2, Z1[2]: 3}.get(n))
                    if n == Z1[0] and k == 1:
                        square_sums(8, (0, 1), bank[0], False)
                    if n == Z1[0] and k == 2:
                        square_sums(0, (6, 7), bank[0], True)

            def turn_qk(j, isq):
                pe.wait_ge(qk_normed, 2 * j + isq + 1)
                turn_bank_free()
                for c in range(2):
                    for t in range(TT):
                        last = nc.tensor.transpose(TR[:, c * S + t * P:c * S + t * P + P],
                                                   qn[:, isq, t, c * P:c * P + P], ident)
                last.then_inc(qk_turned, 1)
                turned.append(("qk", 4 * j + 2 * isq + 2))

            turned = []

            def turn_bank_free():
                if turned:
                    kind, count = turned[-1]
                    pe.wait_ge(qk_out if kind == "qk" else p_out, count)

            def head_scores(h):
                j, c, r = h // 4, (h // 2) % 2, DH * (h % 2)
                pe.wait_ge(qk_out, 4 * j + 4)
                if h >= 2:
                    pe.wait_ge(neg_ready, 2 * h - 2)
                nc.tensor.matmul(SC[h % 2][:, 0:P], qT[r:r + DH, j % 2, c, 0:P], kT[r:r + DH, j % 2, c, 0:P],
                                 start=True, stop=True, skip_group_check=True)
                nc.tensor.matmul(SC[h % 2][:, P:P + S], qT[r:r + DH, j % 2, c, P:S], kT[r:r + DH, j % 2, c, :],
                                 start=False, stop=True, skip_group_check=True).then_inc(scored, 1)

            def head_turn(h):
                pe.wait_ge(prob_ready, 2 * h + 2)
                turn_bank_free()
                for i, (a, b) in enumerate(((0, 0), (128, 128), (256, 256))):
                    last = nc.tensor.transpose(TR[:, a:a + P], prob[:, h % 2, b:b + P], ident)
                last.then_inc(p_turned, 1)
                turned.append(("p", h + 1))

            def head_values(h):
                j, r = h // 4, DH * (h % 2)
                pe.wait_ge(p_out, h + 1)
                pe.wait_ge(v_out, j + 1)
                if h % 2 == 0 and h >= 2:
                    pe.wait_ge(oz_ready, h // 2)
                a = DH * (h % 4)
                nc.tensor.matmul(PV[r:r + DH, 0:S], vv[:, j % 2, 0, a:a + DH], pT[:, h % 2, 0:S],
                                 start=True, stop=False, skip_group_check=True)
                nc.tensor.matmul(PV[r:r + DH, P:S], vv[:, j % 2, 1, a:a + DH], pT[:, h % 2, S:S + P],
                                 start=False, stop=True, skip_group_check=True).then_inc(pv_done, 1)

            def attention_step(j, s):
                for quad, at in ((j - 1, s + STEPS), (j, s)):
                    if not 0 <= quad < 4:
                        continue
                    scores, turns, values = head_steps(quad)
                    for i in range(4):
                        if at == scores[i]:
                            head_scores(4 * quad + i)
                        if at == turns[i]:
                            head_turn(4 * quad + i)
                        if at == values[i]:
                            head_values(4 * quad + i)

            pe.wait_ge(const_in, 16)
            for j in range(4):
                for u, n in enumerate((KU[j], QU[j], VU[j])):
                    m = n - 4
                    if m in Z1:
                        pe.wait_ge(sz1_ready, m - Z1[0] + 1)
                    elif m in VU:
                        pe.wait_ge(v_out, VU.index(m) + 1)
                    else:
                        pe.wait_ge(qk_normed, 2 * ((m - KU[0]) // 3) + (m - KU[0]) % 3 + 1)
                    for k in range(KD):
                        s = 8 * u + k
                        if s == KT_AT:
                            turn_qk(j, 0)
                        if j and s == QT_AT - STEPS:
                            turn_qk(j - 1, 1)
                        attention_step(j - 1, s)
                        token_step(n, k)

            pe.wait_ge(qk_normed, 8)
            s = 0
            for i in range(3):
                n = O1[i]
                for kt in range(2):
                    pe.wait_ge(ozlo_ready, 2 * i + kt + 1)
                    arrived(n, kt)
                    for m in [2, 3, 4, 5, 6, 7, 0, 1]:
                        if m % 2 == 0:
                            if s == QT_AT - STEPS:
                                turn_qk(3, 1)
                            attention_step(3, s)
                            s += 1
                        if i == 0 and kt == 0 and m == 0:
                            pe.wait_ge(v_out, 4)
                        last = out_product(n, kt, m, (ya_hi, ya_lo), 2 * i + kt, 0, i == 0 and kt == 0, False)
                last.then_inc(unit_done, 1)
            while s < STEPS + 12:
                attention_step(4, s % STEPS)
                s += 1
            pe.wait_ge(ozlo_ready, 7)
            arrived(O1[3], 0)
            for m in range(KD):
                out_product(O1[3], 0, m, (ya_hi, ya_lo), 6, 0, False, False)
            pe.wait_ge(ozlo_ready, 8)
            arrived(O1[3], 1)
            for m in range(KD):
                last = out_product(O1[3], 1, m, (ya_hi, ya_lo), 7, 0, False, True)
                if m % 2 == 1:
                    last.then_inc(bank_closed if m < KD - 1 else unit_done, 1)


def kernel(x, norm0_g, w_in0, pool_w, pool_scale, conv_w, conv_b, cnorm_g, cnorm_b, w_out0,
           norm1_g, w_in1, q_norm_g, k_norm_g, w_out1):
    import numpy as np
    import concourse.bacc as bacc
    from concourse.bass_utils import run_bass_kernel_spmd

    def tiles(v):
        return np.asarray(v).reshape(KD, P).T

    def columns(wt, c):
        return np.asarray(wt)[0][:, c:c + UC].reshape(KD, P, UC).transpose(1, 0, 2).reshape(P, UNIT)

    def rows(wt, i):
        return np.asarray(wt)[0][2 * P * i:2 * P * (i + 1)].reshape(2, P, D).transpose(1, 0, 2).reshape(P, UNIT)

    units = []
    for i in range(4):
        units += [columns(w_in0, 2 * D + UC * i), columns(w_in0, D + UC * i)]
    units += [columns(w_in0, UC * g) for g in range(4)]
    units += [columns(w_in0, 4 * D + UC * i) for i in range(4)]
    units += [np.asarray(pool_w)[0].reshape(4, 2, P, UC).transpose(2, 0, 1, 3).reshape(P, UNIT)]
    units += [columns(w_in0, 3 * D + UC * i) for i in range(4)]
    units += [rows(w_out0, i) for i in range(8)]
    units += [columns(w_in1, 3 * D + UC * i) for i in range(4)]
    for j in range(4):
        units += [columns(w_in1, D + UC * j), columns(w_in1, UC * j), columns(w_in1, 2 * D + UC * j)]
    units += [rows(w_out1, i) for i in range(4)]
    taps = np.asarray(conv_w)[0].reshape(TAPS, KD, P).transpose(2, 1, 0).reshape(P, KD * TAPS)
    twice = [np.concatenate([np.asarray(g)[0]] * 2)[:, None] for g in (q_norm_g, k_norm_g)]
    vec = np.concatenate([tiles(norm0_g), tiles(pool_scale), tiles(conv_b), tiles(cnorm_g), tiles(cnorm_b),
                          tiles(norm1_g)] + twice + [taps], axis=1)
    t = np.arange(15)
    inv = np.concatenate([1.0 / np.minimum(t + 1, wd) for wd in WINDOWS])
    q, k = np.arange(P)[:, None], np.arange(P)[None, :]
    own = np.where(q >= k, q - k, FAR)
    heads = 2 * np.arange(KD)[None, :] + np.arange(P)[:, None] // DH
    scale = -DH ** -0.5 * 2.0 ** (8.0 * (heads + 1) / HEADS)
    const = np.concatenate([np.broadcast_to(inv, (P, 60)), own, q - k + P, own, np.eye(P), scale], axis=1).astype(np.float32)
    arrays = {
        "xT": np.ascontiguousarray(np.asarray(x)[0].T.reshape(KD, P, S).transpose(1, 0, 2)),
        "w": np.ascontiguousarray(np.stack(units)),
        "vec": np.ascontiguousarray(vec),
        "const": const,
    }
    nc = bacc.Bacc("TRN2", target_bir_lowering=False, num_devices=1)
    args = [nc.dram_tensor(n, a.shape, F32, kind="ExternalInput").ap() for n, a in arrays.items()]
    out = nc.dram_tensor("out", (P, KD, S), F32, kind="ExternalOutput").ap()
    hybrid_trunk(nc, *args, out)
    r = run_bass_kernel_spmd(nc, [arrays], core_ids=[0])
    return r.results[0]["out"].transpose(1, 0, 2).reshape(D, S).T[None]
```
